# Optimizing a Trainium2 kernel written in Bass

```python
import math
import jax, jax.numpy as jnp
from jax import lax
import numpy as np

D_MODEL = 1024
BATCH = 1
SEQ = 1024
DEPTH = 2

GRID_W = 64
CTX_LEN = 256

N_MIXERS = 4
MIX_CONV, MIX_NAT, MIX_MLA, MIX_FNET = 0, 1, 2, 3
N_MOD = 6

FFN_HIDDEN = -(-8 * D_MODEL // (3 * 256)) * 256

NA_HEADS = 16
NA_HEAD_DIM = D_MODEL // NA_HEADS
NA_WIN_ROWS = 8
NA_WIN_COLS = 16

MLA_HEADS = 16
MLA_Q_RANK = D_MODEL // 4
MLA_KV_RANK = D_MODEL // 4
MLA_NOPE = 64
MLA_ROPE = 32
MLA_V = 64

FNET_GROUPS = 4

ROPE_BASE = 10000.0
NORM_EPS = 1e-6
Q_BLOCK = 128

kernel_name = "hybrid_interleaved_diffusion_trunk"

def rmsnorm(x, g):
    x32 = x.astype(jnp.float32)
    y = x32 * lax.rsqrt(jnp.mean(x32 * x32, axis=-1, keepdims=True) + NORM_EPS)
    return y.astype(x.dtype) * g

def modulate(h, shift, scale):
    return h * (1 + scale) + shift

def axial_rope_tables(n_tokens, rot_dim):
    n_freq = rot_dim // 4
    freq = ROPE_BASE ** (-jnp.arange(n_freq, dtype=jnp.float32) / n_freq)
    t = jnp.arange(n_tokens)
    row = (t // GRID_W).astype(jnp.float32)
    col = (t % GRID_W).astype(jnp.float32)
    ang = jnp.concatenate([row[:, None] * freq, col[:, None] * freq], axis=-1)
    return jnp.cos(ang), jnp.sin(ang)

def apply_rope(x, cos, sin):
    half = x.shape[-1] // 2
    x1, x2 = x[..., :half], x[..., half:]
    return jnp.concatenate([x1 * cos - x2 * sin, x1 * sin + x2 * cos], axis=-1).astype(x.dtype)

def blocked_attention(q, k, v, scale):
    B, Sq, H, dq = q.shape
    nb = Sq // Q_BLOCK
    qb = q.reshape(B, nb, Q_BLOCK, H, dq).transpose(1, 0, 2, 3, 4)

    def one_block(q_blk):
        s = jnp.einsum('bqhd,bkhd->bhqk', q_blk, k).astype(jnp.float32) * scale
        p = jax.nn.softmax(s, axis=-1).astype(v.dtype)
        return jnp.einsum('bhqk,bkhd->bqhd', p, v)

    o = lax.map(one_block, qb)
    return o.transpose(1, 0, 2, 3, 4).reshape(B, Sq, H, v.shape[-1])

def swiglu(h, w_in, w_out):
    gate, up = jnp.split(h @ w_in, 2, axis=-1)
    return (jax.nn.silu(gate) * up) @ w_out

def short_conv_mixer(h, w_in, conv_w, w_out):
    b_gate, c_gate, v = jnp.split(h @ w_in, 3, axis=-1)
    u = c_gate * v
    up = jnp.pad(u, ((0, 0), (1, 1), (0, 0)))
    z = conv_w[0] * up[:, :-2] + conv_w[1] * up[:, 1:-1] + conv_w[2] * up[:, 2:]
    return (b_gate * z) @ w_out

def neighbourhood_attention(hl, hc, w_qkv, rpb, w_o, want_ctx):
    B, S, D = hl.shape
    H, dh = NA_HEADS, NA_HEAD_DIM
    rows = S // GRID_W
    kr = min(NA_WIN_ROWS, rows)
    kc = NA_WIN_COLS
    scale = dh ** -0.5

    qkv = hl @ w_qkv
    to_grid = lambda t: t.reshape(B, rows, GRID_W, H, dh).transpose(0, 3, 1, 2, 4)
    qg, kg, vg = to_grid(qkv[..., :D]), to_grid(qkv[..., D:2 * D]), to_grid(qkv[..., 2 * D:])

    kv_c = hc @ w_qkv[:, D:]
    k_ctx = kv_c[..., :D].reshape(B, -1, H, dh)
    v_ctx = kv_c[..., D:].reshape(B, -1, H, dh)

    cols = jnp.arange(GRID_W)
    c0 = jnp.clip(cols - kc // 2, 0, GRID_W - kc)
    col_idx = c0[:, None] + jnp.arange(kc)
    col_bias = rpb[:, :, col_idx - cols[:, None] + NA_WIN_COLS - 1]

    def row_block(r):
        r0 = jnp.clip(r - kr // 2, 0, rows - kr)
        q_r = lax.dynamic_index_in_dim(qg, r, axis=2, keepdims=False)
        k_band = lax.dynamic_slice_in_dim(kg, r0, kr, axis=2)
        v_band = lax.dynamic_slice_in_dim(vg, r0, kr, axis=2)
        k_win = k_band[:, :, :, col_idx]
        v_win = v_band[:, :, :, col_idx]
        row_off = r0 + jnp.arange(kr) - r + NA_WIN_ROWS - 1
        bias = jnp.take(col_bias, row_off, axis=1).transpose(0, 2, 1, 3)
        s_win = (jnp.einsum('bhqd,bhrqcd->bhqrc', q_r, k_win).astype(jnp.float32) * scale
                 + bias[None].astype(jnp.float32))
        s_ctx = jnp.einsum('bhqd,bkhd->bhqk', q_r, k_ctx).astype(jnp.float32) * scale
        s = jnp.concatenate([s_win.reshape(B, H, GRID_W, kr * kc), s_ctx], axis=-1)
        p = jax.nn.softmax(s, axis=-1).astype(v_win.dtype)
        p_win = p[..., :kr * kc].reshape(B, H, GRID_W, kr, kc)
        p_ctx = p[..., kr * kc:]
        return (jnp.einsum('bhqrc,bhrqcd->bhqd', p_win, v_win)
                + jnp.einsum('bhqk,bkhd->bhqd', p_ctx, v_ctx))

    o = lax.map(row_block, jnp.arange(rows))
    yl = o.transpose(1, 0, 3, 2, 4).reshape(B, S, D) @ w_o

    yc = None
    if want_ctx:
        q_ctx = (hc @ w_qkv[:, :D]).reshape(B, -1, H, dh)
        yc = blocked_attention(q_ctx, k_ctx, v_ctx, scale).reshape(B, -1, D) @ w_o
    return yl, yc

def mla_queries(h, w_dq, q_g, w_uq):
    B, S, _ = h.shape
    q = (rmsnorm(h @ w_dq, q_g) @ w_uq).reshape(B, S, MLA_HEADS, MLA_NOPE + MLA_ROPE)
    return q[..., :MLA_NOPE], q[..., MLA_NOPE:]

def mla_keys_values(h, w_dkv, kv_g, w_ukv):
    B, S, _ = h.shape
    ckv = h @ w_dkv
    c_kv = rmsnorm(ckv[..., :MLA_KV_RANK], kv_g)
    k_rope = ckv[..., MLA_KV_RANK:]
    kv = (c_kv @ w_ukv).reshape(B, S, MLA_HEADS, MLA_NOPE + MLA_V)
    return kv[..., :MLA_NOPE], k_rope, kv[..., MLA_NOPE:]

def mla_join(nope, rope):
    if rope.ndim == 3:
        rope = jnp.broadcast_to(rope[:, :, None, :], nope.shape[:3] + (rope.shape[-1],))
    return jnp.concatenate([nope, rope], axis=-1)

def latent_attention(hl, hc, w_dq, q_g, w_uq, w_dkv, kv_g, w_ukv, w_o, cos, sin, want_ctx):
    B, S, _ = hl.shape
    scale = (MLA_NOPE + MLA_ROPE) ** -0.5
    qn, qr = mla_queries(hl, w_dq, q_g, w_uq)
    kn, kr, v = mla_keys_values(hl, w_dkv, kv_g, w_ukv)
    q_l = mla_join(qn, apply_rope(qr, cos[:, None, :], sin[:, None, :]))
    k_l = mla_join(kn, apply_rope(kr, cos, sin))
    kn_c, kr_c, v_c = mla_keys_values(hc, w_dkv, kv_g, w_ukv)
    k_c = mla_join(kn_c, kr_c)
    k_all = jnp.concatenate([k_l, k_c], axis=1)
    v_all = jnp.concatenate([v, v_c], axis=1)
    yl = blocked_attention(q_l, k_all, v_all, scale).reshape(B, S, MLA_HEADS * MLA_V) @ w_o
    yc = None
    if want_ctx:
        qn_c, qr_c = mla_queries(hc, w_dq, q_g, w_uq)
        o_c = blocked_attention(mla_join(qn_c, qr_c), k_c, v_c, scale)
        yc = o_c.reshape(B, -1, MLA_HEADS * MLA_V) @ w_o
    return yl, yc

def fourier_mixer(h, w_o):
    B, S, D = h.shape
    hg = h.astype(jnp.float32).reshape(B, S, FNET_GROUPS, D // FNET_GROUPS)
    f = jnp.fft.fftn(hg, axes=(1, 3), norm="ortho").real
    return f.reshape(B, S, D).astype(h.dtype) @ w_o

def setup_inputs(seed: int = 0) -> dict:
    key = jax.random.key(seed)
    ks = iter(jax.random.split(key, 32))
    D, F = D_MODEL, FFN_HIDDEN
    n_conv = len(range(MIX_CONV, DEPTH, N_MIXERS))
    n_nat = len(range(MIX_NAT, DEPTH, N_MIXERS))
    n_mla = len(range(MIX_MLA, DEPTH, N_MIXERS))
    n_fnet = len(range(MIX_FNET, DEPTH, N_MIXERS))

    def nrm(shape, scale):
        return jax.random.normal(next(ks), shape, jnp.float32) * scale

    def gain(shape):
        return 1.0 + nrm(shape, 0.05)

    return {
        "x": nrm((BATCH, SEQ, D), 1.0),
        "c": nrm((BATCH, D), 1.0),
        "ctx": nrm((BATCH, CTX_LEN, D), 1.0),
        "c_ctx": nrm((D,), 1.0),
        "mod_w": nrm((DEPTH, D, N_MOD * D), 0.5 * D ** -0.5),
        "mod_b": nrm((DEPTH, N_MOD * D), 0.02),
        "mix_norm_g": gain((DEPTH, D)),
        "ffn_norm_g": gain((DEPTH, D)),
        "conv_w_in": nrm((n_conv, D, 3 * D), D ** -0.5),
        "conv_w": nrm((n_conv, 3, D), 3 ** -0.5),
        "conv_w_out": nrm((n_conv, D, D), D ** -0.5),
        "nat_w_qkv": nrm((n_nat, D, 3 * D), D ** -0.5),
        "nat_rpb": nrm((n_nat, NA_HEADS, 2 * NA_WIN_ROWS - 1, 2 * NA_WIN_COLS - 1), 0.1),
        "nat_w_o": nrm((n_nat, D, D), D ** -0.5),
        "mla_w_dq": nrm((n_mla, D, MLA_Q_RANK), D ** -0.5),
        "mla_q_norm_g": gain((n_mla, MLA_Q_RANK)),
        "mla_w_uq": nrm((n_mla, MLA_Q_RANK, MLA_HEADS * (MLA_NOPE + MLA_ROPE)), MLA_Q_RANK ** -0.5),
        "mla_w_dkv": nrm((n_mla, D, MLA_KV_RANK + MLA_ROPE), D ** -0.5),
        "mla_kv_norm_g": gain((n_mla, MLA_KV_RANK)),
        "mla_w_ukv": nrm((n_mla, MLA_KV_RANK, MLA_HEADS * (MLA_NOPE + MLA_V)), MLA_KV_RANK ** -0.5),
        "mla_w_o": nrm((n_mla, MLA_HEADS * MLA_V, D), (MLA_HEADS * MLA_V) ** -0.5),
        "fnet_w_o": nrm((n_fnet, D, D), D ** -0.5),
        "ffn_w_in": nrm((DEPTH, D, 2 * F), D ** -0.5),
        "ffn_w_out": nrm((DEPTH, F, D), F ** -0.5),
        "final_norm_g": gain((D,)),
    }

def reference(x, c, ctx, c_ctx, mod_w, mod_b, mix_norm_g, ffn_norm_g, conv_w_in, conv_w,
              conv_w_out, nat_w_qkv, nat_rpb, nat_w_o, mla_w_dq, mla_q_norm_g, mla_w_uq,
              mla_w_dkv, mla_kv_norm_g, mla_w_ukv, mla_w_o, fnet_w_o, ffn_w_in, ffn_w_out,
              final_norm_g):
    S = x.shape[1]
    rope_cos, rope_sin = axial_rope_tables(S, MLA_ROPE)
    silu_c = jax.nn.silu(c)
    silu_cc = jax.nn.silu(c_ctx)
    xl, xc = x, ctx
    for i in range(DEPTH):
        kind, j = i % N_MIXERS, i // N_MIXERS
        reads_ctx = kind in (MIX_NAT, MIX_MLA)
        ctx_needed = any((l % N_MIXERS) in (MIX_NAT, MIX_MLA) for l in range(i + 1, DEPTH))

        mod_l = jnp.split(silu_c @ mod_w[i] + mod_b[i], N_MOD, axis=-1)
        sh1, sc1, g1, sh2, sc2, g2 = [m[:, None, :] for m in mod_l]
        hl = modulate(rmsnorm(xl, mix_norm_g[i]), sh1, sc1)
        hc = None
        if reads_ctx or ctx_needed:
            mc = jnp.split(silu_cc @ mod_w[i] + mod_b[i], N_MOD, axis=-1)
            hc = modulate(rmsnorm(xc, mix_norm_g[i]), mc[0], mc[1])

        if kind == MIX_CONV:
            yl = short_conv_mixer(hl, conv_w_in[j], conv_w[j], conv_w_out[j])
            yc = short_conv_mixer(hc, conv_w_in[j], conv_w[j], conv_w_out[j]) if ctx_needed else None
        elif kind == MIX_NAT:
            yl, yc = neighbourhood_attention(hl, hc, nat_w_qkv[j], nat_rpb[j], nat_w_o[j], ctx_needed)
        elif kind == MIX_MLA:
            yl, yc = latent_attention(hl, hc, mla_w_dq[j], mla_q_norm_g[j], mla_w_uq[j], mla_w_dkv[j],
                                      mla_kv_norm_g[j], mla_w_ukv[j], mla_w_o[j], rope_cos, rope_sin,
                                      ctx_needed)
        else:
            yl = fourier_mixer(hl, fnet_w_o[j])
            yc = fourier_mixer(hc, fnet_w_o[j]) if ctx_needed else None

        xl = xl + g1 * yl
        xl = xl + g2 * swiglu(modulate(rmsnorm(xl, ffn_norm_g[i]), sh2, sc2), ffn_w_in[i], ffn_w_out[i])
        if ctx_needed:
            xc = xc + mc[2] * yc
            xc = xc + mc[5] * swiglu(modulate(rmsnorm(xc, ffn_norm_g[i]), mc[3], mc[4]),
                                     ffn_w_in[i], ffn_w_out[i])
    return rmsnorm(xl, final_norm_g)


_drawn_inputs = setup_inputs


def setup_inputs(seed=0):
    import zlib

    import numpy as np

    out = dict(_drawn_inputs(seed))
    spreads = {}
    factors = {'ffn_norm_g': 2.804, 'nat_rpb': 45.414, 'ctx': 38.704, 'c_ctx': 8.0}
    for name, (base, spread) in spreads.items():
        noise = np.random.default_rng([zlib.crc32(name.encode()), seed]).standard_normal(out[name].shape)
        drawn = base * np.exp(spread * noise) if base else spread * noise
        out[name] = __import__('jax').numpy.asarray(drawn.astype(out[name].dtype))
    for name, factor in factors.items():
        out[name] = (out[name] * factor).astype(out[name].dtype)
    return out
```

```python
from contextlib import ExitStack

import concourse.bass as bass
from concourse import mybir

F32 = mybir.dt.float32
F32R = mybir.dt.float32r
ALU = mybir.AluOpType
ACT = mybir.ActivationFunctionType

P = 128
BANK = 512
N_MOD = 6
GRID_W = 64
WIN_ROWS, WIN_COLS = 8, 16
EPS = 1e-6
MASKED = -1e30
SLOTS = 4


def at_least(engine, semaphore, value):
    if not isinstance(value, int) or value > 0:
        engine.wait_ge(semaphore, value)


def token_tiles(tokens):
    return [(t, min(BANK, tokens - t)) for t in range(0, tokens, BANK)]


def trunk(nc, x_t, ctx_t, c_t, mod_panels, mod_bias, norm_gains, conv_panels, conv_taps, ffn_panels,
          v_panels, qk_panels, wo_panels, rpb_padded, out_t):
    D = x_t.shape[0] * x_t.shape[1]
    KB = D // P
    TL, TC = x_t.shape[2], ctx_t.shape[2]
    T = TL + TC
    HIDDEN = ffn_panels.shape[1]
    HEADS = rpb_padded.shape[0]
    DH = D // HEADS
    PAIRS = D // P
    REL = rpb_padded.shape[1]
    PADW = rpb_padded.shape[2]
    SCALE = float(DH) ** -0.5
    CTX_TILES = TC // P
    TOK_TILES = T // P
    MODS = N_MOD * KB
    ROWS = TL // GRID_W
    assert P == 2 * DH == 2 * GRID_W and ROWS == 2 * WIN_ROWS and CTX_TILES == 2 and KB == 8

    with ExitStack() as ctx:
        top = [(nc.sbuf_base + 63) // 64 * 64]

        def place(name, shape, dtype, at=None):
            size = 4
            for n in shape[1:]:
                size *= n
            size = (size + 31) // 32 * 32
            if at is None:
                at = top[0]
                top[0] += size
            return nc.alloc_sbuf_tensor_at(name, shape, dtype, offset=at), at + size

        def keep(name, shape, dtype=F32):
            return place(name, shape, dtype)[0]

        residual = keep("residual", [P, KB, T])
        act_at = top[0]
        act_hi = keep("act_hi", [P, KB, T], F32R)
        act_lo = keep("act_lo", [P, KB, T], F32R)
        raw = keep("raw", [P, SLOTS, D])
        w_hi = keep("w_hi", [P, SLOTS, KB, P], F32R)
        w_lo = keep("w_lo", [P, SLOTS, KB, P], F32R)
        scratch_at = top[0]
        prod_hi = keep("prod_hi", [P, T], F32R)
        prod_lo = keep("prod_lo", [P, T], F32R)
        prod = keep("prod", [P, T + 4])
        gate = keep("gate", [P, T])
        padded = keep("padded", [P, T + 4])
        scratch_end = top[0]
        modulation = keep("modulation", [P, 2 * MODS, 2])
        mod_bias_sb = keep("mod_bias_sb", [P, 2 * MODS])
        gains = keep("gains", [P, 5, KB])
        taps = keep("taps", [P, 3, KB])
        cond = keep("cond", [P, KB, 2])
        silu_c = keep("silu_c", [P, KB, 2])
        norm_scale = keep("norm_scale", [P, 4, KB, 2])
        ident = keep("ident", [P, P])
        ones = keep("ones", [P, P])
        col_mask = keep("col_mask", [P, GRID_W])
        mod_rows = keep("mod_rows", [2, 2, BANK])
        eps_col = keep("eps_col", [P, 1])
        credit = keep("credit", [P, 4])
        spare = top[0]

        squares = padded[:, 0:2 * BANK].rearrange("p (b n) -> p b n", b=2)
        centred = prod[:, 0:2 * BANK].rearrange("p (b n) -> p b n", b=2)
        rstd = gate[:, 0:2 * BANK].rearrange("p (b n) -> p b n", b=2)
        stage_k_hi, _ = place("stage_k_hi", [P, T], F32, scratch_at)
        stage_k_lo, _ = place("stage_k_lo", [P, T], F32, scratch_at + 4 * T)
        stage_q_hi, _ = place("stage_q_hi", [P, TL], F32, scratch_at + 8 * T)
        stage_q_lo, _ = place("stage_q_lo", [P, TL], F32, scratch_at + 12 * T)
        stage_v_hi, _ = place("stage_v_hi", [P, 2, 2 * P], F32, scratch_at)
        stage_v_lo, _ = place("stage_v_lo", [P, 2, 2 * P], F32, scratch_at + 8 * T)

        o_hi, nxt = place("o_hi", [P, PAIRS, TL], F32R, act_at)
        o_lo, nxt = place("o_lo", [P, PAIRS, TL], F32R, nxt)
        q_st, nxt = place("q_st", [P, 2, TL], F32R, nxt)
        k_hi, nxt = place("k_hi", [P, 2, T], F32R, nxt)
        k_lo, nxt = place("k_lo", [P, 2, T], F32R, nxt)
        v_st, nxt = place("v_st", [P, 2, TOK_TILES, P], F32R, nxt)
        bias_full, nxt = place("bias_full", [P, 2, 16, GRID_W], F32, nxt)
        NB = WIN_ROWS + 1
        bias_inner, nxt = place("bias_inner", [P, 2, NB, GRID_W], F32, nxt)
        KEYS_IN, KEYS_OUT = TC + NB * GRID_W, TC + WIN_ROWS * GRID_W
        neg_s, nxt = place("neg_s", [P, 2, KEYS_IN], F32, nxt)
        probs, nxt = place("probs", [P, 4, KEYS_IN + GRID_W], F32, nxt)
        pt_hi, nxt = place("pt_hi", [P, 9, 2 * P], F32R, nxt)
        pt_lo, nxt = place("pt_lo", [P, 9, 2 * P], F32R, nxt)
        assert nxt <= scratch_end, (nxt, scratch_end)
        zeros, spare = place("zeros", [P, TC], F32, spare)
        row_mask, spare = place("row_mask", [P, NB, GRID_W], F32, spare)
        o_half, spare = place("o_half", [P, 2 * P], F32, spare)
        o_sum, spare = place("o_sum", [P, 2 * P], F32, spare)
        stats, spare = place("stats", [P, 4, 4], F32, spare)
        assert spare <= nc.sbuf_usable_end, (spare, nc.sbuf_usable_end)

        psum = ctx.enter_context(nc.psum_tensor("psum", [P, 8, BANK], F32))

        q_dram = [nc.dram_tensor(f"q_dram{n}", [PAIRS, P, TL], F32) for n in range(2)]
        k_dram = [nc.dram_tensor(f"k_dram{n}", [PAIRS, P, T], F32) for n in range(2)]
        v_dram = [nc.dram_tensor(f"v_dram{n}", [HEADS, TOK_TILES, P, DH], F32) for n in range(2)]
        bias_dram = nc.dram_tensor("bias_dram", [HEADS, GRID_W, REL, GRID_W], F32)

        def sem(name):
            return ctx.enter_context(nc.semaphore(name))

        x_in = sem("x_in")
        small_in = sem("small_in")
        bias_in = sem("bias_in")
        consts = sem("consts")
        raw_in = [sem(f"raw_in{s}") for s in range(SLOTS)]
        hi_done = [sem(f"hi_done{s}") for s in range(SLOTS)]
        lo_done = [sem(f"lo_done{s}") for s in range(SLOTS)]
        silu_done = sem("silu_done")
        mod_raw_used = [sem(f"mod_raw_used{s}") for s in range(SLOTS)]
        mod_raw_in = [sem(f"mod_raw_in{s}") for s in range(SLOTS)]
        mod_copied = sem("mod_copied")
        mod_turned = sem("mod_turned")
        mod_ready = sem("mod_ready")

        class NormSems:
            def __init__(self, n):
                self.squared = sem(f"squared{n}")
                self.summed = sem(f"summed{n}")
                self.rooted = sem(f"rooted{n}")
                self.inverted = sem(f"inverted{n}")
                self.scaled = sem(f"scaled{n}")
                self.shifted = sem(f"shifted{n}")
                self.hi = sem(f"hi{n}")
                self.lo_dve = sem(f"lo_dve{n}")
                self.lo_pool = sem(f"lo_pool{n}")

        norms = [NormSems(n) for n in range(5)]
        scales_done = sem("scales_done")
        pool_step = sem("pool_step")
        pe_passed, dve_passed, pool_passed = sem("pe_passed"), sem("dve_passed"), sem("pool_passed")
        CONSTS = 7

        class MixSems:
            def __init__(self, n, conv):
                self.a = sem(f"a_ready{n}")
                self.b = sem(f"b_ready{n}")
                self.c = sem(f"c_ready{n}")
                self.a_copied = sem(f"a_copied{n}")
                self.prod = sem(f"prod{n}")
                self.b_used = sem(f"b_used{n}") if conv else self.prod
                self.c_copied = sem(f"c_copied{n}")
                self.tapped = sem(f"tapped{n}")
                self.hi = sem(f"prod_hi{n}")
                self.lo = sem(f"prod_lo{n}")
                self.out = sem(f"out_ready{n}")
                self.added = sem(f"added{n}")

        conv, ffns = MixSems("_conv", True), [MixSems("_ffn0", False), MixSems("_ffn1", False)]
        pads_zeroed = sem("pads_zeroed")
        v_ready, v_hi_done, v_lo_done = sem("v_ready"), sem("v_hi_done"), sem("v_lo_done")
        v_out = [sem("v_out0"), sem("v_out1")]
        q_ready, k_ready = sem("q_ready"), sem("k_ready")
        q_hi_done, q_lo_done = sem("q_hi_done"), sem("q_lo_done")
        k_hi_done, k_lo_done = sem("k_hi_done"), sem("k_lo_done")
        q_out, k_out = sem("q_out"), sem("k_out")
        qk_in = [sem("qk_in0"), sem("qk_in1")]
        v_in = [sem("v_in0"), sem("v_in1")]
        bias_rows_in = [sem("bias_rows_in0"), sem("bias_rows_in1")]
        attn_consts = sem("attn_consts")
        bias_masked, bias_done = sem("bias_masked"), sem("bias_done")
        s_ready, band_done, s_done = sem("s_ready"), sem("band_done"), sem("s_done")
        exp_done, inv_done, probs_done = sem("exp_done"), sem("inv_done"), sem("probs_done")
        pt_ready, pt_hi_done, pt_lo_done = sem("pt_ready"), sem("pt_hi_done"), sem("pt_lo_done")
        pv_ready, half_done, sum_done = sem("pv_ready"), sem("half_done"), sem("sum_done")
        o_hi_done, o_lo_done = sem("o_hi_done"), sem("o_lo_done")
        y_ready, y_added = sem("y_ready"), sem("y_added")
        final_done, final_out = sem("final_done"), sem("final_out")

        POOL_LO = [kb for kb in range(KB) if kb % 4 != 2]
        ALL, LAT = token_tiles(T), token_tiles(TL)
        MOD_STEPS = 2 * MODS // SLOTS

        base = {}
        filled = [0] * SLOTS
        for phase, times in (("conv", (KB,) * 4), ("ffn0", (HIDDEN,) * 3 + (0,)), ("v", (2,) * 4),
                             ("qk", (PAIRS, PAIRS, 0, 0)), ("wo", (2,) * 4), ("ffn1", (HIDDEN,) * 3 + (0,))):
            base[phase] = list(filled)
            filled = [f + t for f, t in zip(filled, times)]

        ROW0 = [(0, 0), (0, 2), (4, 6), (8, 8)]
        C0, C1, BAND = 0, P, TC
        INNER = [[(0, 1, (BAND + P, BAND)), (1, 2, (BAND + 2 * P, BAND + P))],
                 [(2, 3, (BAND + 3 * P, BAND + 2 * P)), (3, "c0", (C0, C0))],
                 [(4, "c1", (C1, C1)), (5, 0, (BAND, None))],
                 [(6, 5, (None, BAND + 4 * P)), (7, 4, (BAND + 4 * P, BAND + 3 * P))]]
        OUTER = [[(0, 0, (BAND, BAND)), (1, 1, (BAND + P, BAND + P))],
                 [(2, 2, (BAND + 2 * P, BAND + 2 * P)), (3, "c0", (C0, C0))],
                 [(4, "c1", (C1, C1)), (8, 3, (BAND + 3 * P, BAND + 3 * P))]]
        GROUPS = [OUTER, INNER, INNER, OUTER]
        UNITS = 8
        group0 = [sum(len(GROUPS[v % 4]) for v in range(u)) for u in range(UNITS + 1)]
        PAIR_GROUPS = group0[UNITS]

        def pt_target(tensor, group):
            slots = [g[0] for g in group]
            if 5 in slots or 6 in slots:
                flat = tensor[:].rearrange("p s q -> p (s q)")
                start = slots[0] * 2 * P + (P if slots[0] == 6 else 0)
                return flat[:, start:start + 3 * P], 3 * P
            return tensor[:, slots[0]:slots[1] + 1:slots[1] - slots[0], :], 4 * P

        def kind_of(t0):
            return 0 if t0 < TL else 1

        def pad_of(t0):
            return 1 + t0 + 2 * kind_of(t0)

        def panel(tensor, s):
            return tensor[:, s].rearrange("p a b -> p (a b)")

        def before(i, u):
            return (i, u - 1) if u else (i - 1, UNITS - 1)

        def unit_row(u, ab):
            rows0 = ROW0[u % 4][ab]
            return rows0, (WIN_ROWS + 1 if u % 4 in (1, 2) else WIN_ROWS)

        block = ctx.enter_context(nc.Block())

        @block.sync
        def _(sp):
            sp.dma_start(cond[:], c_t).then_inc(small_in, 16)
            sp.dma_start(mod_bias_sb[:], mod_bias).then_inc(small_in, 16)
            sp.dma_start(gains[:], norm_gains).then_inc(small_in, 16)
            sp.dma_start(taps[:], conv_taps).then_inc(small_in, 16)

            def mod_load(i):
                for s in range(SLOTS):
                    at_least(sp, mod_raw_used[s], i)
                    sp.dma_start(raw[:, s, :], mod_panels[i * SLOTS + s]).then_inc(mod_raw_in[s], 16)
            mod_load(0)
            sp.dma_start(residual[:, :, 0:TL], x_t.rearrange("k p t -> p k t")).then_inc(x_in, 16)
            sp.dma_start(residual[:, :, TL:T], ctx_t.rearrange("k p t -> p k t")).then_inc(x_in, 16)
            with sp.Fori(1, MOD_STEPS) as i:
                mod_load(i)

            for h in range(HEADS):
                for c in range(0, GRID_W, 32):
                    src = bass.AP(tensor=rpb_padded.tensor, offset=h * REL * PADW + GRID_W - 1 - c,
                                  ap=[[PADW, REL], [-1, 32], [1, GRID_W]])
                    sp.dma_start(bias_dram[h, c:c + 32].rearrange("c r k -> r c k"), src).then_inc(bias_in, 16)

            def load_panel(phase, s, i, source):
                n = base[phase][s] + i
                at_least(sp, hi_done[s], n)
                at_least(sp, lo_done[s], n)
                sp.dma_start(raw[:, s, :], source).then_inc(raw_in[s], 16)

            for s in range(SLOTS):
                sp.wait_ge(mod_raw_used[s], MOD_STEPS)
                load_panel("conv", s, 0, conv_panels[0, s])
            with sp.Fori(1, KB) as j:
                for s in range(4):
                    load_panel("conv", s, j, conv_panels[j, s])
            with sp.Fori(0, HIDDEN) as j:
                for s in range(3):
                    load_panel("ffn0", s, j, ffn_panels[0, j, s])

            for s in range(4):
                load_panel("v", s, 0, v_panels[s])

            def store_v(i, quarter):
                for t in range(TOK_TILES):
                    n = (2 * i + quarter) * TOK_TILES + t
                    sp.wait_ge(v_hi_done, n + 1)
                    sp.wait_ge(v_lo_done, n + 3)
                    for part, stage in enumerate((stage_v_hi, stage_v_lo)):
                        h0 = (2 * i + quarter) * 4
                        sp.dma_start(v_dram[part][h0:h0 + 4, t].rearrange("h p d -> p h d"),
                                     stage[:, t % 2].rearrange("p (h d) -> p h d", d=DH)).then_inc(v_out[t % 2], 16)
                    if t == TOK_TILES // 2 + 1:
                        for s in (0, 1):
                            if i == 0:
                                load_panel("v", 2 * quarter + s, 1, v_panels[4 + 2 * quarter + s])
                            elif quarter == 0:
                                load_panel("qk", s, 0, qk_panels[0, s])
            store_v(0, 0)
            store_v(0, 1)
            store_v(1, 0)
            store_v(1, 1)

            def store_qk(i):
                sp.wait_ge(q_lo_done, len(LAT) * (i + 1))
                sp.dma_start(q_dram[0][i], stage_q_hi[:]).then_inc(q_out, 16)
                sp.dma_start(q_dram[1][i], stage_q_lo[:]).then_inc(q_out, 16)
                sp.wait_ge(k_lo_done, len(ALL) * (i + 1))
                sp.dma_start(k_dram[0][i], stage_k_hi[:]).then_inc(k_out, 16)
                sp.dma_start(k_dram[1][i], stage_k_lo[:]).then_inc(k_out, 16)
            with sp.Fori(1, PAIRS) as i:
                for s in range(2):
                    load_panel("qk", s, i, qk_panels[i, s])
                store_qk(i - 1)
            store_qk(PAIRS - 1)

            sp.wait_ge(q_out, 32 * PAIRS)
            sp.wait_ge(k_out, 32 * PAIRS)
            for n in range(2):
                sp.wait_ge(v_out[n], 16 * 4 * TOK_TILES)
            sp.wait_ge(bias_in, 32 * HEADS)
            sp.wait_ge(k_ready, len(ALL) * PAIRS)

            def load_head(i, b):
                at_least(sp, s_done, 16 * i + 8 * b - 8)
                for part in range(2):
                    sp.dma_start(q_st[part * DH:(part + 1) * DH, b].bitcast(F32),
                                 q_dram[part][i, b * DH:(b + 1) * DH, :]).then_inc(qk_in[b], 16)
                for part, dst in enumerate((k_hi, k_lo)):
                    for half in range(2):
                        sp.dma_start(dst[half * DH:(half + 1) * DH, b].bitcast(F32),
                                     k_dram[part][i, b * DH:(b + 1) * DH, :]).then_inc(qk_in[b], 16)
                sp.dma_start(bias_full[0:GRID_W, b, 1:REL], bias_dram[2 * i + b, :, 1:REL]).then_inc(bias_rows_in[b], 16)
                sp.dma_start(bias_full[GRID_W:P, b, 1:REL], bias_dram[2 * i + b, :, 0:REL - 1]).then_inc(bias_rows_in[b], 16)
                at_least(sp, pv_ready, 8 * i + 4 * b - 4)
                for part in range(2):
                    sp.dma_start(v_st[:, b, :, part * DH:(part + 1) * DH].bitcast(F32),
                                 v_dram[part][2 * i + b].rearrange("t p d -> p t d")).then_inc(v_in[b], 16)
            load_head(0, 0)
            load_head(0, 1)
            with sp.Fori(1, PAIRS) as i:
                load_head(i, 0)
                load_head(i, 1)

            sp.wait_ge(pv_ready, UNITS * PAIRS)
            sp.wait_ge(sum_done, UNITS * PAIRS)
            for p in range(PAIRS):
                load_panel("wo", p % 4, p // 4, wo_panels[p])
            with sp.Fori(0, HIDDEN) as j:
                for s in range(3):
                    load_panel("ffn1", s, j, ffn_panels[1, j, s])
            for b, (t0, tn) in enumerate(LAT):
                for kb in range(KB):
                    sp.wait_ge(final_done, b * KB + kb + 1)
                    sp.dma_start(out_t[kb, :, t0:t0 + tn], residual[:, kb, t0:t0 + tn]).then_inc(final_out, 16)
            sp.wait_ge(final_out, 16 * KB * len(LAT))

        @block.tensor
        def _(pe):
            def mod_rows_of(i, b):
                at_least(pe, mod_copied, i - 1)
                for s in range(SLOTS):
                    pe.wait_ge(mod_raw_in[s], (i + 1) * 16)
                    for kb in range(KB):
                        mm = pe.matmul(psum[0:2, b, s * P:(s + 1) * P], silu_c[:, kb, :],
                                       raw[:, s, kb * P:(kb + 1) * P], start=(kb == 0), stop=(kb == KB - 1))
                    mm.then_inc(mod_raw_used[s], 1)

            def mod_turn(i, b):
                pe.wait_ge(mod_copied, i + 1)
                at_least(pe, mod_ready, i - 1)
                pe.sem_inc(pe_passed, 1)
                for s in range(SLOTS):
                    mm = pe.transpose(psum[:, 2 + b, 2 * s:2 * s + 2], mod_rows[0:2, b, s * P:(s + 1) * P],
                                      ident[0:2, 0:2])
                mm.then_inc(mod_turned, 1)

            pe.wait_ge(silu_done, 1)
            pe.wait_ge(consts, CONSTS)
            mod_rows_of(0, 0)
            mod_rows_of(1, 1)
            mod_turn(0, 0)
            with pe.Fori(1, MOD_STEPS // 2) as i:
                mod_rows_of(2 * i, 0)
                mod_turn(2 * i - 1, 1)
                mod_rows_of(2 * i + 1, 1)
                mod_turn(2 * i, 0)
            mod_turn(MOD_STEPS - 1, 1)
            pe.wait_ge(mod_ready, MOD_STEPS)

            def norm_sums(n, tiles, b):
                for kb in range(KB):
                    q = b * KB + kb
                    pe.wait_ge(norms[n].squared, q + 1)
                    pe.matmul(psum[:, 3 + b, 0:tiles[b][1]], ones[:], squares[:, q % 2, 0:tiles[b][1]],
                              start=(kb == 0), stop=(kb == KB - 1)).then_inc(norms[n].summed, 1)

            def wait_norm(n, b):
                pe.wait_ge(norms[n].lo_pool, len(POOL_LO) * (b + 1))
                pe.wait_ge(norms[n].lo_dve, (KB - len(POOL_LO)) * (b + 1))

            def project(phase, s, i, bank, tiles, ready, extra=lambda kb: None, acts=(act_hi, act_lo)):
                pe.wait_ge(lo_done[s], base[phase][s] + i + 1)
                for kb in range(KB):
                    for n, (w, h) in enumerate(((w_hi, 0), (w_hi, 1), (w_lo, 0))):
                        for b, (t0, tn) in enumerate(tiles):
                            mm = pe.matmul(psum[:, bank + b, 0:tn], w[:, s, kb, :], acts[h][:, kb, t0:t0 + tn],
                                           start=(kb == 0 and n == 0), stop=(kb == KB - 1 and n == 2))
                            if kb == KB - 1 and n == 2:
                                mm.then_inc(ready, 1)
                    extra(kb)

            def project_behind_norm(n, phase, slots, banks, tiles, readies):
                norm_sums(n, tiles, 0)
                for b, (t0, tn) in enumerate(tiles):
                    if b + 1 < len(tiles):
                        norm_sums(n, tiles, b + 1)
                    wait_norm(n, b)
                    for s, bank, ready in zip(slots, banks, readies):
                        pe.wait_ge(lo_done[s], base[phase][s] + 1)
                        project_tile(s, bank + b, t0, tn).then_inc(ready, 1)

            def project_tile(s, bank, t0, tn):
                for kb in range(KB):
                    for n, (w, h) in enumerate(((w_hi, act_hi), (w_hi, act_lo), (w_lo, act_hi))):
                        mm = pe.matmul(psum[:, bank, 0:tn], w[:, s, kb, :], h[:, kb, t0:t0 + tn],
                                       start=(kb == 0 and n == 0), stop=(kb == KB - 1 and n == 2))
                return mm

            def out_piece(m, s, ob, r, j, count, t0, tn):
                pe.wait_ge(m.added, j * count + r + 1)
                for n, (w, h) in enumerate(((w_hi, prod_hi), (w_hi, prod_lo), (w_lo, prod_hi))):
                    mm = pe.matmul(psum[:, 6 + r % 2, 0:tn], w[:, s, ob, :], h[:, t0:t0 + tn],
                                   start=(n == 0), stop=(n == 2))
                mm.then_inc(m.out, 1)

            def out_block(m, phase, s, ob, j, tiles):
                if ob == 0:
                    pe.wait_ge(lo_done[s], base[phase][s] + j + 1)
                    pe.wait_ge(m.lo, len(tiles) * (j + 1))
                for b, (t0, tn) in enumerate(tiles):
                    out_piece(m, s, ob, ob * len(tiles) + b, j, KB * len(tiles), t0, tn)

            def out_last(m, phase, s, j, tiles):
                pe.wait_ge(lo_done[s], base[phase][s] + j + 1)
                pe.wait_ge(m.lo, len(tiles) * (j + 1))
                for b, (t0, tn) in enumerate(tiles):
                    for ob in range(KB):
                        out_piece(m, s, ob, b * KB + ob, j, KB * len(tiles), t0, tn)

            def conv_step(j):
                prev = not (isinstance(j, int) and j == 0)
                if prev:
                    at_least(pe, conv.c_copied, len(ALL) * j)
                    project("conv", 0, j, 0, ALL, conv.a,
                            lambda kb: out_block(conv, "conv", 3, {4: 0, 6: 1}[kb], j - 1, ALL) if kb in (4, 6) else None)
                    pe.wait_ge(conv.b_used, len(ALL) * j)
                    project("conv", 1, j, 3, ALL, conv.b,
                            lambda kb: out_block(conv, "conv", 3, {1: 2, 4: 3}[kb], j - 1, ALL) if kb in (1, 4) else None)
                    pe.wait_ge(conv.a_copied, len(ALL) * (j + 1))
                    project("conv", 2, j, 0, ALL, conv.c,
                            lambda kb: out_block(conv, "conv", 3, {1: 4, 4: 5}[kb], j - 1, ALL) if kb in (1, 4) else None)
                    out_block(conv, "conv", 3, 6, j - 1, ALL)
                    out_block(conv, "conv", 3, 7, j - 1, ALL)
                else:
                    project_behind_norm(0, "conv", (0, 1), (0, 3), ALL, (conv.a, conv.b))
                    pe.wait_ge(conv.a_copied, len(ALL))
                    project("conv", 2, j, 0, ALL, conv.c)
            conv_step(0)
            with pe.Fori(1, KB) as j:
                conv_step(j)
            out_last(conv, "conv", 3, KB - 1, ALL)

            def ffn_step(m, phase, n, tiles, j):
                if isinstance(j, int) and j == 0:
                    project_behind_norm(n, phase, (0, 1), (0, 3), tiles, (m.a, m.b))
                    return
                pe.wait_ge(m.a_copied, len(tiles) * j)
                project(phase, 0, j, 0, tiles, m.a,
                        lambda kb: out_block(m, phase, 2, kb - 4, j - 1, tiles) if kb >= 4 else None)
                pe.wait_ge(m.b_used, len(tiles) * j)
                project(phase, 1, j, 3, tiles, m.b,
                        lambda kb: out_block(m, phase, 2, 4 + kb // 2, j - 1, tiles) if kb % 2 == 0 else None)

            ffn_step(ffns[0], "ffn0", 1, ALL, 0)
            with pe.Fori(1, HIDDEN) as j:
                ffn_step(ffns[0], "ffn0", 1, ALL, j)
            out_last(ffns[0], "ffn0", 2, HIDDEN - 1, ALL)

            def v_quarter(i, quarter):
                for s in (2 * quarter, 2 * quarter + 1):
                    pe.wait_ge(lo_done[s], base["v"][s] + i + 1)
                for t in range(TOK_TILES):
                    pe.wait_ge(v_lo_done, (2 * i + quarter) * TOK_TILES + t + 1)
                    if i == quarter == 0 and t * P % BANK == 0:
                        wait_norm(2, t * P // BANK)
                    for kb in range(KB):
                        for n, (h, w) in enumerate(((act_hi, w_hi), (act_lo, w_hi), (act_hi, w_lo))):
                            mm = pe.matmul(psum[:, t % 2, 0:2 * P], h[:, kb, t * P:(t + 1) * P],
                                           w[:, 2 * quarter:2 * quarter + 2, kb, :],
                                           start=(kb == 0 and n == 0), stop=(kb == KB - 1 and n == 2))
                    mm.then_inc(v_ready, 1)
            for b in range(len(ALL)):
                norm_sums(2, ALL, b)
            for i in range(2):
                v_quarter(i, 0)
                v_quarter(i, 1)

            def qk_step(i):
                at_least(pe, q_lo_done, len(LAT) * i)
                if isinstance(i, int):
                    pe.wait_ge(v_lo_done, 4 * TOK_TILES + 2)
                project("qk", 0, i, 0, LAT, q_ready)
                at_least(pe, k_lo_done, len(ALL) * i)
                project("qk", 1, i, 3, ALL, k_ready)
            qk_step(0)
            with pe.Fori(1, PAIRS) as i:
                qk_step(i)

            def scores(i, u, ab):
                b = u // 4
                if u % 4 == 0 and ab == 0:
                    pe.wait_ge(qk_in[b], 96 * (i + 1))
                at_least(pe, s_done, 16 * i + 2 * u + ab - 1)
                q0 = (4 * (u % 4) + 2 * ab) * GRID_W
                row0, rows = unit_row(u, ab)
                k0 = row0 * GRID_W
                rest = rows * GRID_W - TC
                for bank, col, key, n in ((0, 0, TL, TC), (0, TC, k0, TC), (1, 0, k0 + TC, rest)):
                    for part, k in enumerate((k_hi, k_lo)):
                        mm = pe.matmul(psum[:, 2 * ab + bank, col:col + n], q_st[:, b, q0:q0 + P],
                                       k[:, b, key:key + n], start=(part == 0), stop=(part == 1))
                mm.then_inc(s_ready, 1)

            def turn(i, u, g):
                n = PAIR_GROUPS * i + group0[u] + g
                at_least(pe, pt_lo_done, n - 1)
                if g == 0:
                    pe.wait_ge(probs_done, 16 * i + 2 * u + 2)
                col = 0
                for slot, _, starts in GROUPS[u % 4][g]:
                    for ab, start in enumerate(starts):
                        if start is not None:
                            mm = pe.transpose(psum[:, 4 + (group0[u] + g) % 2, col:col + P],
                                              probs[:, 2 * (u % 2) + ab, start:start + P], ident[:])
                            col += P
                mm.then_inc(pt_ready, 1)

            def values(i, u, g):
                if g == 0:
                    at_least(pe, sum_done, UNITS * i + u - 1)
                    if u % 4 == 0:
                        pe.wait_ge(v_in[u // 4], 32 * (i + 1))
                pe.wait_ge(pt_lo_done, PAIR_GROUPS * i + group0[u] + g + 1)
                groups = GROUPS[u % 4]
                tile0 = ROW0[u % 4][0] * GRID_W // P
                for m, (slot, key, _) in enumerate(groups[g]):
                    tile = {"c0": TL // P, "c1": TL // P + 1}.get(key, tile0 + key if isinstance(key, int) else 0)
                    for part, pt in enumerate((pt_hi, pt_lo)):
                        mm = pe.matmul(psum[:, 6 + u % 2, 0:2 * P], v_st[:, u // 4, tile, :], pt[:, slot, :],
                                       start=(g == 0 and m == 0 and part == 0),
                                       stop=(g == len(groups) - 1 and m == 1 and part == 1))
                if g == len(groups) - 1:
                    mm.then_inc(pv_ready, 1)

            def attention(i, last):
                for u in range(UNITS):
                    n = len(GROUPS[u % 4])
                    for g in range(n):
                        if g + 2 < n:
                            turn(i, u, g + 2)
                        elif u < UNITS - 1:
                            turn(i, u + 1, g + 2 - n)
                        elif not last:
                            turn(i + 1, 0, g + 2 - n)
                        if g < 2:
                            if u + 2 < UNITS:
                                scores(i, u + 2, g)
                            elif not last:
                                scores(i + 1, u + 2 - UNITS, g)
                        values(i, u, g)
            pe.wait_ge(attn_consts, 5)
            pe.wait_ge(q_lo_done, len(LAT) * PAIRS)
            pe.wait_ge(k_lo_done, len(ALL) * PAIRS)
            for u in range(2):
                for ab in range(2):
                    scores(0, u, ab)
            turn(0, 0, 0)
            turn(0, 0, 1)
            attention(0, False)
            with pe.Fori(1, PAIRS - 1) as i:
                attention(i, False)
            attention(PAIRS - 1, True)

            pe.wait_ge(o_lo_done, UNITS * PAIRS)
            for p in range(PAIRS):
                at_least(pe, y_added, len(LAT) * (p - 1))
                project("wo", p % 4, p // 4, 2 * (p % 2), LAT, y_ready, acts=(o_hi, o_lo))

            pe.wait_ge(y_added, len(LAT) * PAIRS)
            ffn_step(ffns[1], "ffn1", 3, LAT, 0)
            with pe.Fori(1, HIDDEN) as j:
                ffn_step(ffns[1], "ffn1", 3, LAT, j)
            out_last(ffns[1], "ffn1", 2, HIDDEN - 1, LAT)
            for b in range(len(LAT)):
                norm_sums(4, LAT, b)

        @block.scalar
        def _(act):
            act.wait_ge(small_in, 64)
            act.activation(silu_c[:], cond[:], ACT.Silu).then_inc(silu_done, 1)

            def split_hi(phase, s, i, waits=()):
                for semaphore, value in waits:
                    act.wait_ge(semaphore, value)
                n = base[phase][s] + i
                act.wait_ge(raw_in[s], (n + 1) * 16)
                act.activation(panel(w_hi, s), raw[:, s], ACT.Copy).then_inc(hi_done[s], 1)

            def norm(n, tiles, ready):
                m = norms[n]

                def high(b, kb):
                    t0, tn = tiles[b]
                    q = b * KB + kb
                    act.wait_ge(m.shifted, q + 1)
                    act.activation(act_hi[:, kb, t0:t0 + tn], centred[:, q % 2, 0:tn],
                                   ACT.Copy).then_inc(m.hi, 1)

                for b, (t0, tn) in enumerate(tiles):
                    ready(b)
                    for kb in range(KB):
                        q = b * KB + kb
                        at_least(act, m.summed, q - 1)
                        act.activation(squares[:, q % 2, 0:tn], residual[:, kb, t0:t0 + tn],
                                       ACT.Square).then_inc(m.squared, 1)
                        if b > 0 and n < 4:
                            high(b - 1, kb)
                    act.wait_ge(m.summed, KB * (b + 1))
                    act.activation(rstd[:, b % 2, 0:tn], psum[:, 3 + b, 0:tn], ACT.Sqrt, bias=eps_col[:, 0:1],
                                   scale=1.0 / D).then_inc(m.rooted, 1)
                if n < 4:
                    for kb in range(KB):
                        high(len(tiles) - 1, kb)

            act.wait_ge(consts, CONSTS)
            for s in range(3):
                split_hi("conv", s, 0)
            norm(0, ALL, lambda b: act.wait_ge(x_in, 32))

            def product_high(m, j, tiles, padding=False):
                at_least(act, m.out, KB * len(tiles) * j)
                for b, (t0, tn) in enumerate(tiles):
                    act.wait_ge(m.prod, len(tiles) * j + b + 1)
                    at = pad_of(t0) if padding else t0
                    act.activation(prod_hi[:, t0:t0 + tn], prod[:, at:at + tn], ACT.Copy).then_inc(m.hi, 1)

            def conv_step(j, last=False):
                n = len(ALL)
                at_least(act, conv.prod, n * j)
                for b, (t0, tn) in enumerate(ALL):
                    act.wait_ge(conv.a, n * j + b + 1)
                    act.activation(gate[:, t0:t0 + tn], psum[:, b, 0:tn], ACT.Copy).then_inc(conv.a_copied, 1)
                split_hi("conv", 0, j + 1)
                split_hi("conv", 1, j + 1, [(conv.b, n * j + n)])
                for b, (t0, tn) in enumerate(ALL):
                    act.wait_ge(conv.c, n * j + b + 1)
                    act.wait_ge(conv.b_used, n * j + b + 1)
                    act.activation(gate[:, t0:t0 + tn], psum[:, b, 0:tn], ACT.Copy).then_inc(conv.c_copied, 1)
                if not last:
                    split_hi("conv", 2, j + 1)
                product_high(conv, j, ALL, padding=True)
                split_hi("conv", 3, j)

            conv_step(0)
            with act.Fori(1, KB - 1) as j:
                conv_step(j)
            conv_step(KB - 1, last=True)

            def ffn_step(m, phase, tiles, j, last=False):
                n = len(tiles)
                at_least(act, m.prod, n * j)
                for b, (t0, tn) in enumerate(tiles):
                    act.wait_ge(m.a, n * j + b + 1)
                    act.activation(gate[:, t0:t0 + tn], psum[:, b, 0:tn], ACT.Silu).then_inc(m.a_copied, 1)
                if not last:
                    split_hi(phase, 0, j + 1)
                    split_hi(phase, 1, j + 1, [(m.b, n * j + n)])
                product_high(m, j, tiles)
                split_hi(phase, 2, j)

            done = KB * len(ALL)
            norm(1, ALL, lambda b: act.wait_ge(conv.added, done * (KB - 1) + KB * (b + 1) + 2))
            ffn_step(ffns[0], "ffn0", ALL, 0)
            with act.Fori(1, HIDDEN) as j:
                ffn_step(ffns[0], "ffn0", ALL, j)

            norm(2, ALL, lambda b: act.wait_ge(ffns[0].added, done * (HIDDEN - 1) + KB * (b + 1) + 2))
            for quarter in range(4):
                for t in range(TOK_TILES):
                    n = quarter * TOK_TILES + t
                    act.wait_ge(v_ready, n + 1)
                    at_least(act, v_out[t % 2], 32 * (n // 2))
                    act.activation(stage_v_hi[:, t % 2].bitcast(F32R), psum[:, t % 2, 0:2 * P],
                                   ACT.Copy).then_inc(v_hi_done, 1)
                    if t == TOK_TILES // 2 - 1:
                        for s in ((2, 3) if quarter % 2 == 0 else (0, 1)):
                            split_hi("v", s, (quarter + 1) // 2)

            def qk_step(i, last=False):
                at_least(act, q_out, 32 * i)
                for b, (t0, tn) in enumerate(LAT):
                    act.wait_ge(q_ready, len(LAT) * i + b + 1)
                    act.activation(stage_q_hi[:, t0:t0 + tn].bitcast(F32R), psum[:, b, 0:tn], ACT.Copy,
                                   scale=SCALE).then_inc(q_hi_done, 1)
                if not last:
                    split_hi("qk", 0, i + 1)
                at_least(act, k_out, 32 * i)
                for b, (t0, tn) in enumerate(ALL):
                    act.wait_ge(k_ready, len(ALL) * i + b + 1)
                    act.activation(stage_k_hi[:, t0:t0 + tn].bitcast(F32R), psum[:, 3 + b, 0:tn],
                                   ACT.Copy).then_inc(k_hi_done, 1)
                if not last:
                    split_hi("qk", 1, i + 1)
            for n in range(2):
                act.wait_ge(v_out[n], 16 * 4 * TOK_TILES)
            qk_step(0)
            with act.Fori(1, PAIRS - 1) as i:
                qk_step(i)
            qk_step(PAIRS - 1, last=True)

            def exponentials(i, u, ab):
                n = 16 * i + 2 * u + ab
                keys = TC + unit_row(u, ab)[1] * GRID_W
                pb = 2 * (u % 2) + ab
                act.wait_ge(s_done, n + 1)
                act.activation(probs[:, pb, 0:keys], neg_s[:, ab, 0:keys], ACT.Exp, bias=stats[:, pb, 1:2],
                               scale=-1.0, accum_out=stats[:, pb, 2:3]).then_inc(exp_done, 1)

            def pt_high(i, u, g):
                act.wait_ge(pt_ready, PAIR_GROUPS * i + group0[u] + g + 1)
                dst, n = pt_target(pt_hi, GROUPS[u % 4][g])
                src = psum[:, 4 + (group0[u] + g) % 2, 0:n]
                if n == 4 * P:
                    src = src.rearrange("p (s q) -> p s q", s=2)
                act.activation(dst, src, ACT.Copy).then_inc(pt_hi_done, 1)

            def half(i, u):
                act.wait_ge(pv_ready, UNITS * i + u + 1)
                at_least(act, sum_done, UNITS * i + u)
                act.activation(o_half[0:DH, :], psum[DH:P, 6 + u % 2, 0:2 * P], ACT.Copy).then_inc(half_done, 1)

            def out_high(i, u):
                h0, q0 = DH * (u // 4), 4 * (u % 4) * GRID_W
                act.wait_ge(sum_done, UNITS * i + u + 1)
                act.activation(o_hi[h0:h0 + DH, i, q0:q0 + 2 * P], o_sum[h0:h0 + DH, :], ACT.Copy).then_inc(o_hi_done, 1)

            def attention(i, last):
                first = isinstance(i, int) and i == 0
                for u in range(UNITS):
                    nxt_i, nxt_u = (i, u + 1) if u < UNITS - 1 else (i + 1, 0)
                    more = not (last and u == UNITS - 1)
                    if more:
                        exponentials(nxt_i, nxt_u, 0)
                    pt_high(i, u, 0)
                    if more:
                        exponentials(nxt_i, nxt_u, 1)
                    pt_high(i, u, 1)
                    if not (first and u == 0):
                        half(*before(i, u))
                    pt_high(i, u, 2)
                    if not (first and u == 0):
                        out_high(*before(i, u))
                    if len(GROUPS[u % 4]) == 4:
                        pt_high(i, u, 3)
            act.wait_ge(attn_consts, 2)
            act.wait_ge(qk_in[0], 96)
            exponentials(0, 0, 0)
            exponentials(0, 0, 1)
            attention(0, False)
            with act.Fori(1, PAIRS - 1) as i:
                attention(i, False)
            attention(PAIRS - 1, True)
            half(PAIRS - 1, UNITS - 1)
            out_high(PAIRS - 1, UNITS - 1)

            for s in range(4):
                split_hi("wo", s, 0)
            for p in range(PAIRS - 2):
                s = p % 4
                split_hi("wo", s, p // 4 + 1, [(y_ready, len(LAT) * (p + 1))])
            norm(3, LAT, lambda b: act.wait_ge(y_added, len(LAT) * PAIRS))
            ffn_step(ffns[1], "ffn1", LAT, 0)
            with act.Fori(1, HIDDEN - 1) as j:
                ffn_step(ffns[1], "ffn1", LAT, j)
            ffn_step(ffns[1], "ffn1", LAT, HIDDEN - 1, last=True)
            done_lat = KB * len(LAT)
            norm(4, LAT, lambda b: act.wait_ge(ffns[1].added, done_lat * (HIDDEN - 1) + KB * (b + 1) + 2))

        @block.vector
        def _(dve):
            dve.memset(eps_col[:], EPS).then_inc(consts, 1)
            dve.memset(padded[:], 0.0).then_inc(pads_zeroed, 1)
            dve.wait_ge(small_in, 64)

            def mod_copy(i, b):
                at_least(dve, mod_turned, i - 1)
                dve.wait_ge(mod_raw_used[SLOTS - 1], i + 1)
                dve.tensor_copy(mod_rows[:, b, :], psum[0:2, b, :]).then_inc(mod_copied, 1)

            def mod_column(i, b):
                dve.wait_ge(mod_turned, i + 1)
                bias = mod_bias_sb[:, bass.ds(i * SLOTS, SLOTS)]
                for c in range(2):
                    ins = dve.tensor_tensor(modulation[:, bass.ds(i * SLOTS, SLOTS), c],
                                            psum[:, 2 + b, c:2 * SLOTS:2], bias, ALU.add)
                ins.then_inc(mod_ready, 1)

            mod_copy(0, 0)
            mod_copy(1, 1)
            mod_column(0, 0)
            with dve.Fori(1, MOD_STEPS // 2) as i:
                mod_copy(2 * i, 0)
                mod_column(2 * i - 1, 1)
                mod_copy(2 * i + 1, 1)
                mod_column(2 * i, 0)
            mod_column(MOD_STEPS - 1, 1)
            dve.wait_ge(mod_ready, MOD_STEPS)
            for n in range(4):
                first = (n // 2) * MODS + (n % 2) * 3 * KB
                for c in range(2):
                    dve.scalar_tensor_tensor(out=norm_scale[:, n, :, c], in0=modulation[:, first + KB:first + 2 * KB, c],
                                             scalar=1.0, in1=gains[:, n, :], op0=ALU.add,
                                             op1=ALU.mult).then_inc(scales_done, 1)
            dve.wait_ge(scales_done, 8)

            def norm(n, tiles):
                m = norms[n]
                first = (n // 2) * MODS + (n % 2) * 3 * KB
                pool_lo = lambda q: (q // KB) * len(POOL_LO) + len([k for k in POOL_LO if k <= q % KB])
                own_lo = lambda q: q + 1 - pool_lo(q)

                def low(b, kb):
                    t0, tn = tiles[b]
                    q = b * KB + kb
                    dve.wait_ge(m.hi, q + 1)
                    dve.tensor_tensor(act_lo[:, kb, t0:t0 + tn], centred[:, q % 2, 0:tn],
                                      act_hi[:, kb, t0:t0 + tn], ALU.subtract).then_inc(m.lo_dve, 1)

                for b, (t0, tn) in enumerate(tiles):
                    kind = kind_of(t0)
                    dve.wait_ge(m.rooted, b + 1)
                    dve.reciprocal(rstd[:, b % 2, 0:tn], rstd[:, b % 2, 0:tn]).then_inc(m.inverted, 1)
                    dve.wait_ge(m.inverted, b + 1)
                    for kb in range(KB):
                        q = b * KB + kb
                        if q > 1:
                            dve.wait_ge(m.hi, q - 1)
                            dve.wait_ge(m.lo_pool, pool_lo(q - 2))
                            at_least(dve, m.lo_dve, own_lo(q - 2))
                        dve.tensor_tensor(centred[:, q % 2, 0:tn], residual[:, kb, t0:t0 + tn],
                                          rstd[:, b % 2, 0:tn], ALU.mult).then_inc(m.scaled, 1)
                        dve.wait_ge(m.scaled, q + 1)
                        dve.tensor_scalar(centred[:, q % 2, 0:tn], centred[:, q % 2, 0:tn],
                                          norm_scale[:, n, kb, kind:kind + 1],
                                          modulation[:, first + kb, kind:kind + 1],
                                          ALU.mult, ALU.add).then_inc(m.shifted, 1)
                        if (kb - 1) % KB not in POOL_LO and kb > 0:
                            low(b, kb - 1)
                    if KB - 1 not in POOL_LO:
                        low(b, KB - 1)
                dve.wait_ge(m.hi, KB * len(tiles))
                dve.wait_ge(m.lo_pool, pool_lo(KB * len(tiles) - 1))
                at_least(dve, m.lo_dve, own_lo(KB * len(tiles) - 1))

            def add_piece(m, ob, r, j, count, t0, tn, gates):
                dve.wait_ge(m.out, j * count + r + 1)
                dve.scalar_tensor_tensor(out=residual[:, ob, t0:t0 + tn], in0=psum[:, 6 + r % 2, 0:tn],
                                         scalar=modulation[:, gates + ob, kind_of(t0):kind_of(t0) + 1],
                                         in1=residual[:, ob, t0:t0 + tn],
                                         op0=ALU.mult, op1=ALU.add).then_inc(m.added, 1)

            def add_block(m, ob, j, tiles, gates):
                for b, (t0, tn) in enumerate(tiles):
                    add_piece(m, ob, ob * len(tiles) + b, j, KB * len(tiles), t0, tn, gates)

            def add_last(m, j, tiles, gates):
                dve.wait_ge(m.added, j * KB * len(tiles) + 2)
                for b, (t0, tn) in enumerate(tiles):
                    for ob in range(KB):
                        add_piece(m, ob, b * KB + ob, j, KB * len(tiles), t0, tn, gates)

            def product_low(m, j, tiles, padding=False):
                for b, (t0, tn) in enumerate(tiles):
                    dve.wait_ge(m.hi, len(tiles) * j + b + 1)
                    at = pad_of(t0) if padding else t0
                    dve.tensor_tensor(prod_lo[:, t0:t0 + tn], prod[:, at:at + tn], prod_hi[:, t0:t0 + tn],
                                      ALU.subtract).then_inc(m.lo, 1)

            for n, m in enumerate((conv, *ffns)):
                dve.memset(credit[:, n:n + 1], 0.0).then_inc(m.added, 2)
            dve.memset(credit[:, 3:4], 0.0).then_inc(v_lo_done, 2)
            norm(0, ALL)
            dve.wait_ge(norms[0].summed, KB * len(ALL))
            dve.memset(padded[:], 0.0).then_inc(pads_zeroed, 1)
            dve.wait_ge(pads_zeroed, 2)

            def conv_step(j):
                n, gates = len(ALL), 2 * KB
                some = not isinstance(j, int)
                if some:
                    for ob in range(4):
                        add_block(conv, ob, j - 1, ALL, gates)
                for b, (t0, tn) in enumerate(ALL):
                    dve.wait_ge(conv.a_copied, n * j + b + 1)
                    dve.wait_ge(conv.b, n * j + b + 1)
                    at = pad_of(t0)
                    dve.tensor_tensor(padded[:, at:at + tn], psum[:, 3 + b, 0:tn], gate[:, t0:t0 + tn],
                                      ALU.mult).then_inc(conv.b_used, 1)
                dve.wait_ge(conv.b_used, n * j + n)
                at_least(dve, conv.hi, n * j)
                at_least(dve, conv.lo, n * j)
                inside = slice(1, T + 3)
                dve.tensor_scalar(prod[:, inside], padded[:, inside], taps[:, 1, bass.ds(j, 1)], None,
                                  ALU.mult).then_inc(conv.tapped, 1)
                dve.wait_ge(conv.tapped, 3 * j + 1)
                for shift, tap in ((0, 0), (2, 2)):
                    dve.scalar_tensor_tensor(out=prod[:, inside], in0=padded[:, shift:shift + T + 2],
                                             scalar=taps[:, tap, bass.ds(j, 1)], in1=prod[:, inside],
                                             op0=ALU.mult, op1=ALU.add).then_inc(conv.tapped, 1)
                    dve.wait_ge(conv.tapped, 3 * j + 2 + tap // 2)
                if some:
                    for ob in range(4, KB):
                        add_block(conv, ob, j - 1, ALL, gates)
                for b, (t0, tn) in enumerate(ALL):
                    at = pad_of(t0)
                    dve.wait_ge(conv.c_copied, n * j + b + 1)
                    dve.tensor_tensor(prod[:, at:at + tn], prod[:, at:at + tn], gate[:, t0:t0 + tn],
                                      ALU.mult).then_inc(conv.prod, 1)
                product_low(conv, j, ALL, padding=True)

            conv_step(0)
            with dve.Fori(1, KB) as j:
                conv_step(j)
            add_last(conv, KB - 1, ALL, 2 * KB)

            def ffn_step(m, tiles, j, gates):
                n = len(tiles)
                if not (isinstance(j, int) and j == 0):
                    for ob in range(KB):
                        add_block(m, ob, j - 1, tiles, gates)
                at_least(dve, m.hi, n * j)
                at_least(dve, m.lo, n * j)
                for b, (t0, tn) in enumerate(tiles):
                    dve.wait_ge(m.a_copied, n * j + b + 1)
                    dve.wait_ge(m.b, n * j + b + 1)
                    dve.tensor_tensor(prod[:, t0:t0 + tn], psum[:, 3 + b, 0:tn], gate[:, t0:t0 + tn],
                                      ALU.mult).then_inc(m.prod, 1)
                product_low(m, j, tiles)

            norm(1, ALL)
            ffn_step(ffns[0], ALL, 0, 5 * KB)
            with dve.Fori(1, HIDDEN) as j:
                ffn_step(ffns[0], ALL, j, 5 * KB)
            add_last(ffns[0], HIDDEN - 1, ALL, 5 * KB)

            norm(2, ALL)
            for n in range(4 * TOK_TILES):
                at_least(dve, v_out[n % 2], 32 * (n // 2))
                dve.wait_ge(v_hi_done, n + 1)
                dve.tensor_tensor(stage_v_lo[:, n % 2].bitcast(F32R), psum[:, n % 2, 0:2 * P],
                                  stage_v_hi[:, n % 2], ALU.subtract).then_inc(v_lo_done, 1)

            def qk_step(i):
                at_least(dve, q_out, 32 * i)
                for b, (t0, tn) in enumerate(LAT):
                    dve.wait_ge(q_hi_done, len(LAT) * i + b + 1)
                    dve.scalar_tensor_tensor(out=stage_q_lo[:, t0:t0 + tn].bitcast(F32R), in0=psum[:, b, 0:tn],
                                             scalar=SCALE, in1=stage_q_hi[:, t0:t0 + tn], op0=ALU.mult,
                                             op1=ALU.subtract).then_inc(q_lo_done, 1)
                at_least(dve, k_out, 32 * i)
                for b, (t0, tn) in enumerate(ALL):
                    dve.wait_ge(k_hi_done, len(ALL) * i + b + 1)
                    dve.tensor_tensor(stage_k_lo[:, t0:t0 + tn].bitcast(F32R), psum[:, 3 + b, 0:tn],
                                      stage_k_hi[:, t0:t0 + tn], ALU.subtract).then_inc(k_lo_done, 1)
            for n in range(2):
                dve.wait_ge(v_out[n], 16 * 4 * TOK_TILES)
            qk_step(0)
            with dve.Fori(1, PAIRS) as i:
                qk_step(i)

            dve.wait_ge(q_out, 32 * PAIRS)
            dve.wait_ge(k_out, 32 * PAIRS)
            dve.wait_ge(k_ready, len(ALL) * PAIRS)
            dve.memset(probs[:], 0.0).then_inc(attn_consts, 1)
            dve.memset(pt_hi[:, 5:7, :].bitcast(F32), 0.0).then_inc(attn_consts, 1)
            dve.memset(pt_lo[:, 5:7, :].bitcast(F32), 0.0).then_inc(attn_consts, 1)
            dve.memset(zeros[:], 0.0).then_inc(attn_consts, 1)
            dve.memset(stats[:], 0.0).then_inc(attn_consts, 1)
            dve.wait_ge(attn_consts, 5)

            def bias_scores(i, u, ab):
                n = 16 * i + 2 * u + ab
                b, pb = u // 4, 2 * (u % 2) + ab
                row0, rows = unit_row(u, ab)
                if ab == 0 and u % 4 == 0:
                    dve.wait_ge(bias_done, 2 * i + b + 1)
                if rows > WIN_ROWS:
                    table = bias_inner[:, b]
                else:
                    e0 = row0 - (4 * (u % 4) + 2 * ab) + WIN_ROWS - 1
                    table = bias_full[:, b, e0:e0 + rows]
                band = rows * GRID_W
                both = psum[:, 2 * ab:2 * ab + 2, :].rearrange("p b n -> p (b n)")
                dve.wait_ge(s_ready, n + 1)
                at_least(dve, exp_done, n - 1)
                dve.sem_inc(dve_passed, 1)
                dve.tensor_tensor_reduce(neg_s[:, ab, TC:TC + band], both[:, TC:TC + band],
                                         table.rearrange("p r c -> p (r c)"), -1.0, 3e38, ALU.add, ALU.min,
                                         stats[:, pb, 0:1]).then_inc(band_done, 1)
                dve.wait_ge(band_done, n + 1)
                dve.sem_inc(dve_passed, 1)
                dve.tensor_tensor_reduce(neg_s[:, ab, 0:TC], both[:, 0:TC], zeros[:], -1.0, stats[:, pb, 0:1],
                                         ALU.add, ALU.min, stats[:, pb, 1:2]).then_inc(s_done, 1)

            def invert(i, u, ab):
                n, pb = 16 * i + 2 * u + ab, 2 * (u % 2) + ab
                dve.wait_ge(exp_done, n + 1)
                dve.reciprocal(stats[:, pb, 3:4], stats[:, pb, 2:3]).then_inc(inv_done, 1)

            def pt_low(i, u, g):
                dst, n = pt_target(pt_lo, GROUPS[u % 4][g])
                hi, _ = pt_target(pt_hi, GROUPS[u % 4][g])
                src = psum[:, 4 + (group0[u] + g) % 2, 0:n]
                if n == 4 * P:
                    src = src.rearrange("p (s q) -> p s q", s=2)
                dve.wait_ge(pt_hi_done, PAIR_GROUPS * i + group0[u] + g + 1)
                dve.tensor_tensor(dst, src, hi, ALU.subtract).then_inc(pt_lo_done, 1)

            def head_sum(i, u):
                n = UNITS * i + u
                h0 = DH * (u // 4)
                dve.wait_ge(half_done, n + 1)
                at_least(dve, o_hi_done, n)
                at_least(dve, o_lo_done, n)
                dve.tensor_tensor(o_sum[h0:h0 + DH, :], psum[0:DH, 6 + u % 2, 0:2 * P], o_half[0:DH, :],
                                  ALU.add).then_inc(sum_done, 1)

            def attention(i, last):
                first = isinstance(i, int) and i == 0
                for u in range(UNITS):
                    nxt_i, nxt_u = (i, u + 1) if u < UNITS - 1 else (i + 1, 0)
                    far_i, far_u = (i, u + 2) if u + 2 < UNITS else (i + 1, u + 2 - UNITS)
                    pt_low(i, u, 0)
                    if not (last and u == UNITS - 1):
                        invert(nxt_i, nxt_u, 0)
                    pt_low(i, u, 1)
                    if not (last and u == UNITS - 1):
                        invert(nxt_i, nxt_u, 1)
                    if not (first and u == 0):
                        head_sum(*before(i, u))
                    if not (last and far_u < 2):
                        bias_scores(far_i, far_u, 0)
                    pt_low(i, u, 2)
                    if not (last and far_u < 2):
                        bias_scores(far_i, far_u, 1)
                    if len(GROUPS[u % 4]) == 4:
                        pt_low(i, u, 3)
            bias_scores(0, 0, 0)
            bias_scores(0, 0, 1)
            invert(0, 0, 0)
            bias_scores(0, 1, 0)
            invert(0, 0, 1)
            bias_scores(0, 1, 1)
            attention(0, False)
            with dve.Fori(1, PAIRS - 1) as i:
                attention(i, False)
            attention(PAIRS - 1, True)
            head_sum(PAIRS - 1, UNITS - 1)

            for p in range(PAIRS):
                for b, (t0, tn) in enumerate(LAT):
                    dve.wait_ge(y_ready, len(LAT) * p + b + 1)
                    dve.scalar_tensor_tensor(out=residual[:, p, t0:t0 + tn], in0=psum[:, 2 * (p % 2) + b, 0:tn],
                                             scalar=modulation[:, MODS + 2 * KB + p, 0:1],
                                             in1=residual[:, p, t0:t0 + tn], op0=ALU.mult,
                                             op1=ALU.add).then_inc(y_added, 1)

            norm(3, LAT)
            gates = MODS + 5 * KB
            ffn_step(ffns[1], LAT, 0, gates)
            with dve.Fori(1, HIDDEN) as j:
                ffn_step(ffns[1], LAT, j, gates)
            add_last(ffns[1], HIDDEN - 1, LAT, gates)

            for b, (t0, tn) in enumerate(LAT):
                m = norms[4]
                dve.wait_ge(m.rooted, b + 1)
                dve.reciprocal(rstd[:, b % 2, 0:tn], rstd[:, b % 2, 0:tn]).then_inc(m.inverted, 1)
                dve.wait_ge(m.inverted, b + 1)
                for kb in range(KB):
                    dve.scalar_tensor_tensor(out=residual[:, kb, t0:t0 + tn], in0=residual[:, kb, t0:t0 + tn],
                                             scalar=gains[:, 4, kb:kb + 1], in1=rstd[:, b % 2, 0:tn],
                                             op0=ALU.mult, op1=ALU.mult).then_inc(final_done, 1)

        @block.gpsimd
        def _(pool):
            pool.memset(ident[:], 0.0).then_inc(pool_step, 1)
            pool.memset(col_mask[:], 0.0).then_inc(pool_step, 1)
            pool.memset(row_mask[:], 0.0).then_inc(pool_step, 1)
            pool.memset(ones[:], 1.0).then_inc(consts, 1)
            pool.wait_ge(pool_step, 3)
            pool.affine_select(out=ident[:], in_=ident[:], compare_op=ALU.not_equal, fill=1.0, base=0,
                               pattern=[[-1, P]], channel_multiplier=1).then_inc(consts, 1)
            reach = WIN_COLS // 2
            for half in range(2):
                h = slice(half * GRID_W, (half + 1) * GRID_W)
                left = col_mask[h, 0:GRID_W - WIN_COLS]
                pool.affine_select(out=left, in_=left, compare_op=ALU.is_ge, fill=MASKED, base=reach,
                                   pattern=[[1, GRID_W - WIN_COLS]], channel_multiplier=-1).then_inc(pool_step, 1)
                pool.wait_ge(pool_step, 4 + half)
                right = col_mask[h, WIN_COLS:GRID_W]
                pool.affine_select(out=right, in_=right, compare_op=ALU.is_ge, fill=MASKED,
                                   base=reach - 1 - WIN_COLS, pattern=[[-1, GRID_W - WIN_COLS]],
                                   channel_multiplier=1).then_inc(consts, 1)
            pool.memset(row_mask[0:GRID_W, WIN_ROWS, :], MASKED).then_inc(consts, 1)
            pool.memset(row_mask[GRID_W:P, 0, :], MASKED).then_inc(consts, 1)
            pool.wait_ge(consts, CONSTS)

            def split_lo(phase, s, i):
                pool.wait_ge(hi_done[s], base[phase][s] + i + 1)
                pool.tensor_tensor(panel(w_lo, s), raw[:, s], panel(w_hi, s), ALU.subtract).then_inc(lo_done[s], 1)

            def norm(n, tiles):
                m = norms[n]
                for b, (t0, tn) in enumerate(tiles):
                    for kb in POOL_LO:
                        q = b * KB + kb
                        pool.wait_ge(m.hi, q + 1)
                        pool.tensor_tensor(act_lo[:, kb, t0:t0 + tn], centred[:, q % 2, 0:tn],
                                           act_hi[:, kb, t0:t0 + tn], ALU.subtract).then_inc(m.lo_pool, 1)

            for s in range(3):
                split_lo("conv", s, 0)
            norm(0, ALL)

            def conv_step(j, last=False):
                for s in (0, 1) if last else (0, 1, 2):
                    split_lo("conv", s, j + 1)
                split_lo("conv", 3, j)
            conv_step(0)
            with pool.Fori(1, KB - 1) as j:
                conv_step(j)
            conv_step(KB - 1, last=True)

            def ffn_step(phase, j, last=False):
                for s in () if last else (0, 1):
                    split_lo(phase, s, j + 1)
                split_lo(phase, 2, j)
            norm(1, ALL)
            with pool.Fori(0, HIDDEN) as j:
                ffn_step("ffn0", j)
            norm(2, ALL)
            for quarter in range(4):
                for s in ((2, 3) if quarter % 2 == 0 else (0, 1)):
                    split_lo("v", s, (quarter + 1) // 2)
            with pool.Fori(0, PAIRS - 1) as i:
                for s in range(2):
                    split_lo("qk", s, i + 1)

            def tables(i, b):
                pool.wait_ge(bias_rows_in[b], 32 * (i + 1))
                mask = col_mask[:, None, :]
                pool.tensor_tensor(bias_full[:, b, 1:REL], bias_full[:, b, 1:REL],
                                   mask.to_broadcast([P, REL - 1, GRID_W]), ALU.add).then_inc(bias_masked, 1)
                pool.wait_ge(bias_masked, 2 * i + b + 1)
                e0 = WIN_ROWS // 2 - 1
                pool.tensor_tensor(bias_inner[:, b], bias_full[:, b, e0:e0 + WIN_ROWS + 1], row_mask[:],
                                   ALU.add).then_inc(bias_done, 1)

            def normalise(i, u, ab):
                n, pb = 16 * i + 2 * u + ab, 2 * (u % 2) + ab
                keys = TC + unit_row(u, ab)[1] * GRID_W
                pool.wait_ge(inv_done, n + 1)
                pool.sem_inc(pool_passed, 1)
                pool.tensor_scalar(probs[:, pb, 0:keys], probs[:, pb, 0:keys], stats[:, pb, 3:4], 1.0,
                                   ALU.mult, ALU.mult).then_inc(probs_done, 1)

            def out_low(i, u, started):
                h0, q0 = DH * (u // 4), 4 * (u % 4) * GRID_W
                if h0:
                    pool.wait_ge(probs_done, started)
                pool.wait_ge(o_hi_done, UNITS * i + u + 1)
                pool.tensor_tensor(o_lo[h0:h0 + DH, i, q0:q0 + 2 * P], o_sum[h0:h0 + DH, :],
                                   o_hi[h0:h0 + DH, i, q0:q0 + 2 * P], ALU.subtract).then_inc(o_lo_done, 1)
                if h0:
                    pool.wait_ge(o_lo_done, UNITS * i + u + 1)

            def attention(i, last):
                first = isinstance(i, int) and i == 0
                for u in range(UNITS):
                    nxt_i, nxt_u = (i, u + 1) if u < UNITS - 1 else (i + 1, 0)
                    if u == 0 and not first:
                        tables(i, 1)
                    if u == 4 and not last:
                        tables(i + 1, 0)
                        pool.wait_ge(bias_done, 2 * i + 3)
                    more = not (last and u == UNITS - 1)
                    if more:
                        normalise(nxt_i, nxt_u, 0)
                        normalise(nxt_i, nxt_u, 1)
                    if not (first and u == 0):
                        out_low(*before(i, u), 16 * i + 2 * u + (4 if more else 2))
            tables(0, 0)
            tables(0, 1)
            normalise(0, 0, 0)
            normalise(0, 0, 1)
            attention(0, False)
            with pool.Fori(1, PAIRS - 1) as i:
                attention(i, False)
            attention(PAIRS - 1, True)
            out_low(PAIRS - 1, UNITS - 1, 2 * UNITS * PAIRS)

            for s in range(4):
                split_lo("wo", s, 0)
            for p in range(PAIRS - 2):
                split_lo("wo", p % 4, p // 4 + 1)
            norm(3, LAT)
            with pool.Fori(0, HIDDEN - 1) as j:
                ffn_step("ffn1", j)
            ffn_step("ffn1", HIDDEN - 1, last=True)


def kernel(x, c, ctx, c_ctx, mod_w, mod_b, mix_norm_g, ffn_norm_g, conv_w_in, conv_w, conv_w_out, nat_w_qkv,
           nat_rpb, nat_w_o, mla_w_dq, mla_q_norm_g, mla_w_uq, mla_w_dkv, mla_kv_norm_g, mla_w_ukv, mla_w_o,
           fnet_w_o, ffn_w_in, ffn_w_out, final_norm_g):
    import numpy as np
    from concourse import bacc
    from concourse.bass_utils import run_bass_kernel_spmd

    arr = {n: np.asarray(a) for n, a in dict(
        x=x, c=c, ctx=ctx, c_ctx=c_ctx, mod_w=mod_w, mod_b=mod_b, mix_norm_g=mix_norm_g, ffn_norm_g=ffn_norm_g,
        conv_w_in=conv_w_in, conv_w=conv_w, conv_w_out=conv_w_out, nat_w_qkv=nat_w_qkv, nat_rpb=nat_rpb,
        nat_w_o=nat_w_o, ffn_w_in=ffn_w_in, ffn_w_out=ffn_w_out, final_norm_g=final_norm_g).items()}
    D = arr["x"].shape[-1]
    KB = D // P
    TL, TC = arr["x"].shape[1], arr["ctx"].shape[1]
    F = arr["ffn_w_out"].shape[1]

    def columns(w):
        return w.reshape(KB, P, -1, P).transpose(2, 1, 0, 3).reshape(-1, P, D)

    def per_channel(v):
        return np.moveaxis(v.reshape(*v.shape[:-1], KB, P), -1, 0)

    conv_in = columns(arr["conv_w_in"][0]).reshape(3, KB, P, D)
    conv = np.stack([conv_in[1], conv_in[2], conv_in[0], arr["conv_w_out"][0].reshape(KB, P, D)], 1)
    ffn = []
    for layer in range(2):
        up = columns(arr["ffn_w_in"][layer]).reshape(2, F // P, P, D)
        ffn.append(np.stack([up[0], up[1], arr["ffn_w_out"][layer].reshape(F // P, P, D)], 1))
    qkv = columns(arr["nat_w_qkv"][0]).reshape(3, KB, P, D)
    rpb = arr["nat_rpb"][0]
    side = GRID_W - WIN_COLS
    arrays = {
        "x_t": arr["x"][0].T.reshape(KB, P, TL),
        "ctx_t": arr["ctx"][0].T.reshape(KB, P, TC),
        "c_t": per_channel(np.stack([arr["c"][0], arr["c_ctx"]])).transpose(0, 2, 1),
        "mod_panels": np.concatenate([columns(arr["mod_w"][layer]) for layer in range(2)]),
        "mod_bias": arr["mod_b"].reshape(-1, P).T,
        "norm_gains": per_channel(np.stack([arr["mix_norm_g"][0], arr["ffn_norm_g"][0], arr["mix_norm_g"][1],
                                            arr["ffn_norm_g"][1], arr["final_norm_g"]])),
        "conv_panels": conv,
        "conv_taps": per_channel(arr["conv_w"][0]),
        "ffn_panels": np.stack(ffn),
        "v_panels": qkv[2],
        "qk_panels": np.stack([qkv[0], qkv[1]], 1),
        "wo_panels": columns(arr["nat_w_o"][0]),
        "rpb_padded": np.pad(rpb, ((0, 0), (0, 0), (side, side))),
    }
    nc = bacc.Bacc("TRN2", target_bir_lowering=False, num_devices=1)
    arrays = {n: np.ascontiguousarray(a) for n, a in arrays.items()}
    args = [nc.dram_tensor(n, a.shape, F32, kind="ExternalInput").ap() for n, a in arrays.items()]
    out = nc.dram_tensor("out_t", (KB, P, TL), F32, kind="ExternalOutput").ap()
    trunk(nc, *args, out)
    r = run_bass_kernel_spmd(nc, [arrays], core_ids=[0])
    return np.ascontiguousarray(r.results[0]["out_t"].reshape(D, TL).T)[None]
```

```python
from contextlib import ExitStack

import concourse.bass as bass
from concourse import mybir

F32 = mybir.dt.float32
F32R = mybir.dt.float32r
ALU = mybir.AluOpType
ACT = mybir.ActivationFunctionType

P = 128
BANK = 512
N_MOD = 6
GRID_W = 64
WIN_ROWS, WIN_COLS = 8, 16
EPS = 1e-6
MASKED = -1e30
SLOTS = 4


def at_least(engine, semaphore, value):
    if not isinstance(value, int) or value > 0:
        engine.wait_ge(semaphore, value)


def token_tiles(tokens):
    return [(t, min(BANK, tokens - t)) for t in range(0, tokens, BANK)]


def trunk(nc, x_t, ctx_t, c_t, mod_panels, mod_rest, mod_bias, norm_gains, conv_panels, conv_taps, ffn_panels,
          v_panels, qk_panels, wo_panels, rpb_padded, out_t):
    D = x_t.shape[0] * x_t.shape[1]
    KB = D // P
    TL, TC = x_t.shape[2], ctx_t.shape[2]
    T = TL + TC
    HIDDEN = ffn_panels.shape[1]
    HEADS = rpb_padded.shape[0]
    DH = D // HEADS
    PAIRS = D // P
    REL = rpb_padded.shape[1]
    PADW = rpb_padded.shape[2]
    SCALE = float(DH) ** -0.5
    CTX_TILES = TC // P
    TOK_TILES = T // P
    MODS = N_MOD * KB
    ROWS = TL // GRID_W
    assert P == 2 * DH == 2 * GRID_W and ROWS == 2 * WIN_ROWS and CTX_TILES == 2 and KB == 8

    with ExitStack() as ctx:
        top = [(nc.sbuf_base + 63) // 64 * 64]

        def place(name, shape, dtype, at=None):
            size = 4
            for n in shape[1:]:
                size *= n
            size = (size + 31) // 32 * 32
            if at is None:
                at = top[0]
                top[0] += size
            return nc.alloc_sbuf_tensor_at(name, shape, dtype, offset=at), at + size

        def keep(name, shape, dtype=F32):
            return place(name, shape, dtype)[0]

        residual = keep("residual", [P, KB, T])
        act_at = top[0]
        act_hi = keep("act_hi", [P, KB, T], F32R)
        act_lo = keep("act_lo", [P, KB, T], F32R)
        raw = keep("raw", [P, SLOTS, D])
        w_hi = keep("w_hi", [P, SLOTS, KB, P], F32R)
        w_lo = keep("w_lo", [P, SLOTS, KB, P], F32R)
        raw_at, w_hi_at, w_lo_at = (act_at + 8 * KB * T + (n * SLOTS + SLOTS - 1) * 4 * D for n in range(3))
        scratch_at = top[0]
        prod_hi = keep("prod_hi", [P, T], F32R)
        prod_lo = keep("prod_lo", [P, T], F32R)
        prod = keep("prod", [P, T + 4])
        gate = keep("gate", [P, T])
        GROUP_COLS = mod_rest.shape[3]
        mod_in = [place(f"mod_in{n}", [P, 2, GROUP_COLS], F32, at)[0] for n, at in enumerate((raw_at, w_hi_at))]
        mod_acc, _ = place("mod_acc", [P, 2, GROUP_COLS], F32, w_lo_at)
        padded = keep("padded", [P, T + 4])
        scratch_end = top[0]
        modulation = keep("modulation", [P, 2 * MODS, 2])
        mod_bias_sb = keep("mod_bias_sb", [P, 2 * MODS])
        gains = keep("gains", [P, 5, KB])
        taps = keep("taps", [P, 3, KB])
        cond = keep("cond", [P, KB, 2])
        silu_c = keep("silu_c", [P, KB, 2])
        norm_scale = keep("norm_scale", [P, 4, KB, 2])
        ident = keep("ident", [P, P])
        ones = keep("ones", [P, P])
        col_mask = keep("col_mask", [P, GRID_W])
        mod_rows = keep("mod_rows", [2, 2, BANK])
        eps_col = keep("eps_col", [P, 1])
        credit = keep("credit", [P, 4])
        spare = top[0]

        squares = padded[:, 0:2 * BANK].rearrange("p (b n) -> p b n", b=2)
        centred = prod[:, 0:2 * BANK].rearrange("p (b n) -> p b n", b=2)
        rstd = gate
        stage_k_hi, _ = place("stage_k_hi", [P, T], F32, scratch_at)
        stage_k_lo, _ = place("stage_k_lo", [P, T], F32, scratch_at + 4 * T)
        stage_q_hi, _ = place("stage_q_hi", [P, TL], F32, scratch_at + 8 * T)
        stage_q_lo, _ = place("stage_q_lo", [P, TL], F32, scratch_at + 12 * T)
        stage_v_hi, _ = place("stage_v_hi", [P, 2, 2 * P], F32, scratch_at)
        stage_v_lo, _ = place("stage_v_lo", [P, 2, 2 * P], F32, scratch_at + 4 * T)

        o_hi, nxt = place("o_hi", [P, PAIRS, TL], F32R, act_at)
        o_lo, nxt = place("o_lo", [P, PAIRS, TL], F32R, nxt)
        q_st, nxt = place("q_st", [P, 2, TL], F32R, nxt)
        k_hi, nxt = place("k_hi", [P, 2, T], F32R, nxt)
        k_lo, nxt = place("k_lo", [P, 2, T], F32R, nxt)
        v_st, nxt = place("v_st", [P, 2, TOK_TILES, P], F32R, nxt)
        bias_full, nxt = place("bias_full", [P, 2, 16, GRID_W], F32, nxt)
        NB = WIN_ROWS + 1
        bias_inner, nxt = place("bias_inner", [P, 2, NB, GRID_W], F32, nxt)
        KEYS_IN, KEYS_OUT = TC + NB * GRID_W, TC + WIN_ROWS * GRID_W
        neg_s, nxt = place("neg_s", [P, 2, KEYS_IN], F32, nxt)
        probs, nxt = place("probs", [P, 4, KEYS_IN + GRID_W], F32, nxt)
        pt_hi, nxt = place("pt_hi", [P, 9, 2 * P], F32R, nxt)
        pt_lo, nxt = place("pt_lo", [P, 9, 2 * P], F32R, nxt)
        assert nxt <= scratch_end, (nxt, scratch_end)
        zeros, spare = place("zeros", [P, TC], F32, spare)
        row_mask, spare = place("row_mask", [P, NB, GRID_W], F32, spare)
        o_half, spare = place("o_half", [P, 2 * P], F32, spare)
        o_sum, spare = place("o_sum", [P, 2 * P], F32, spare)
        stats, spare = place("stats", [P, 4, 4], F32, spare)
        assert spare <= nc.sbuf_usable_end, (spare, nc.sbuf_usable_end)

        psum = ctx.enter_context(nc.psum_tensor("psum", [P, 8, BANK], F32))

        q_dram = [nc.dram_tensor(f"q_dram{n}", [PAIRS, P, TL], F32) for n in range(2)]
        k_dram = [nc.dram_tensor(f"k_dram{n}", [PAIRS, P, T], F32) for n in range(2)]
        v_dram = [nc.dram_tensor(f"v_dram{n}", [HEADS, TOK_TILES, P, DH], F32) for n in range(2)]
        bias_dram = nc.dram_tensor("bias_dram", [HEADS, GRID_W, REL, GRID_W], F32)

        def sem(name):
            return ctx.enter_context(nc.semaphore(name))

        x_in = sem("x_in")
        small_in = sem("small_in")
        bias_in = sem("bias_in")
        consts = sem("consts")
        raw_in = [sem(f"raw_in{s}") for s in range(SLOTS)]
        hi_done = [sem(f"hi_done{s}") for s in range(SLOTS)]
        lo_done = [sem(f"lo_done{s}") for s in range(SLOTS)]
        silu_done = sem("silu_done")
        mod_raw_used = [sem(f"mod_raw_used{s}") for s in range(SLOTS)]
        mod_raw_in = [sem(f"mod_raw_in{s}") for s in range(SLOTS)]
        mod_copied = sem("mod_copied")
        mod_turned = sem("mod_turned")
        mod_ready = sem("mod_ready")
        rest_in = [sem("rest_in0"), sem("rest_in1")]
        rest_acc, rest_summed, rest_ready = sem("rest_acc"), sem("rest_summed"), sem("rest_ready")

        class NormSems:
            def __init__(self, n):
                self.squared = sem(f"squared{n}")
                self.summed = sem(f"summed{n}")
                self.rooted = sem(f"rooted{n}")
                self.inverted = sem(f"inverted{n}")
                if n == 4:
                    return
                self.scaled = sem(f"scaled{n}")
                self.hi = sem(f"hi{n}")
                self.shifted = sem(f"shifted{n}")
                self.lo_dve = sem(f"lo_dve{n}")
                self.lo_pool = sem(f"lo_pool{n}")

        norms = [NormSems(n) for n in range(5)]
        scales_done = sem("scales_done")
        pool_step = sem("pool_step")
        pe_passed, dve_passed, pool_passed = sem("pe_passed"), sem("dve_passed"), sem("pool_passed")
        CONSTS = 7

        class MixSems:
            def __init__(self, n, conv):
                self.a = sem(f"a_ready{n}")
                self.b = sem(f"b_ready{n}")
                if conv:
                    self.c = sem(f"c_ready{n}")
                    self.c_copied = sem(f"c_copied{n}")
                    self.tapped = sem(f"tapped{n}")
                self.a_copied = sem(f"a_copied{n}")
                self.prod = sem(f"prod{n}")
                self.b_used = sem(f"b_used{n}") if conv else self.prod
                self.hi = sem(f"prod_hi{n}")
                self.lo = sem(f"prod_lo{n}")
                self.out = sem(f"out_ready{n}")
                self.added = sem(f"added{n}")

        conv, ffns = MixSems("_conv", True), [MixSems("_ffn0", False), MixSems("_ffn1", False)]
        pads_zeroed = sem("pads_zeroed")
        v_ready, v_hi_done, v_lo_done = sem("v_ready"), sem("v_hi_done"), sem("v_lo_done")
        v_out = [sem("v_out0"), sem("v_out1")]
        q_ready, k_ready = sem("q_ready"), sem("k_ready")
        q_hi_done, q_lo_done = sem("q_hi_done"), sem("q_lo_done")
        k_hi_done, k_lo_done = sem("k_hi_done"), sem("k_lo_done")
        q_out, k_out = sem("q_out"), sem("k_out")
        qk_in = [sem("qk_in0"), sem("qk_in1")]
        v_in = [sem("v_in0"), sem("v_in1")]
        bias_rows_in = [sem("bias_rows_in0"), sem("bias_rows_in1")]
        attn_consts = sem("attn_consts")
        bias_masked, bias_done = sem("bias_masked"), sem("bias_done")
        s_ready, band_done, s_done = sem("s_ready"), sem("band_done"), sem("s_done")
        exp_done, inv_done, probs_done = sem("exp_done"), sem("inv_done"), sem("probs_done")
        pt_ready, pt_hi_done, pt_lo_done = sem("pt_ready"), sem("pt_hi_done"), sem("pt_lo_done")
        pv_ready, half_done, sum_done = sem("pv_ready"), sem("half_done"), sem("sum_done")
        o_hi_done, o_lo_done = sem("o_hi_done"), sem("o_lo_done")
        y_ready, y_added = sem("y_ready"), sem("y_added")
        final_done, final_out = sem("final_done"), sem("final_out")

        POOL_LO = (3, 6)

        def pool_lows(q):
            return q // KB * len(POOL_LO) + len([kb for kb in POOL_LO if kb <= q % KB])

        def wait_lows(engine, m, q):
            at_least(engine, m.lo_pool, pool_lows(q))
            at_least(engine, m.lo_dve, q + 1 - pool_lows(q))

        ALL, LAT = token_tiles(T), token_tiles(TL)
        MOD_STEPS = MODS // SLOTS
        MOD_HALF = MOD_STEPS // 4
        MOD_GROUPS = mod_rest.shape[0]
        GROUP_BLOCKS = GROUP_COLS // P
        GROUP_STEPS = 2 * KB
        assert MOD_GROUPS + 2 < HIDDEN and MOD_GROUPS * GROUP_BLOCKS == MODS

        base = {}
        filled = [0] * SLOTS
        for phase, times in (("conv", (KB,) * 4), ("ffn0", (HIDDEN,) * 3 + (0,)), ("v", (2,) * 4),
                             ("qk", (PAIRS, PAIRS, 0, 0)), ("wo", (2,) * 4), ("ffn1", (HIDDEN,) * 3 + (0,))):
            base[phase] = list(filled)
            filled = [f + t for f, t in zip(filled, times)]

        ROW0 = [(0, 0), (0, 2), (4, 6), (8, 8)]
        C0, C1, BAND = 0, P, TC
        INNER = [[(0, 1, (BAND + P, BAND)), (1, 2, (BAND + 2 * P, BAND + P))],
                 [(2, 3, (BAND + 3 * P, BAND + 2 * P)), (3, "c0", (C0, C0))],
                 [(4, "c1", (C1, C1)), (5, 0, (BAND, None))],
                 [(6, 5, (None, BAND + 4 * P)), (7, 4, (BAND + 4 * P, BAND + 3 * P))]]
        OUTER = [[(0, 0, (BAND, BAND)), (1, 1, (BAND + P, BAND + P))],
                 [(2, 2, (BAND + 2 * P, BAND + 2 * P)), (3, "c0", (C0, C0))],
                 [(4, "c1", (C1, C1)), (8, 3, (BAND + 3 * P, BAND + 3 * P))]]
        GROUPS = [OUTER, INNER, INNER, OUTER]
        UNITS = 8
        group0 = [sum(len(GROUPS[v % 4]) for v in range(u)) for u in range(UNITS + 1)]
        PAIR_GROUPS = group0[UNITS]

        def pt_target(tensor, group):
            slots = [g[0] for g in group]
            if 5 in slots or 6 in slots:
                flat = tensor[:].rearrange("p s q -> p (s q)")
                start = slots[0] * 2 * P + (P if slots[0] == 6 else 0)
                return flat[:, start:start + 3 * P], 3 * P
            return tensor[:, slots[0]:slots[1] + 1:slots[1] - slots[0], :], 4 * P

        V_BANKS = (0, 1, 6, 7)

        def kind_of(t0):
            return 0 if t0 < TL else 1

        def pad_of(t0):
            return 1 + t0 + 2 * kind_of(t0)

        def panel(tensor, s):
            return tensor[:, s].rearrange("p a b -> p (a b)")

        def before(i, u):
            return (i, u - 1) if u else (i - 1, UNITS - 1)

        def unit_row(u, ab):
            rows0 = ROW0[u % 4][ab]
            return rows0, (WIN_ROWS + 1 if u % 4 in (1, 2) else WIN_ROWS)

        block = ctx.enter_context(nc.Block())

        @block.sync
        def _(sp):
            sp.dma_start(cond[:], c_t).then_inc(small_in, 16)
            sp.dma_start(mod_bias_sb[:], mod_bias).then_inc(small_in, 16)
            sp.dma_start(gains[:], norm_gains).then_inc(small_in, 16)
            sp.dma_start(taps[:], conv_taps).then_inc(small_in, 16)

            def mod_load(i):
                for s in range(SLOTS):
                    at_least(sp, mod_raw_used[s], i)
                    sp.dma_start(raw[:, s, :], mod_panels[i * SLOTS + s]).then_inc(mod_raw_in[s], 16)
            mod_load(0)
            sp.dma_start(residual[:, :, 0:TL], x_t.rearrange("k p t -> p k t")).then_inc(x_in, 16)
            sp.dma_start(residual[:, :, TL:T], ctx_t.rearrange("k p t -> p k t")).then_inc(x_in, 16)
            with sp.Fori(1, MOD_STEPS) as i:
                mod_load(i)

            def load_panel(phase, s, i, source):
                n = base[phase][s] + i
                at_least(sp, hi_done[s], n)
                at_least(sp, lo_done[s], n)
                sp.dma_start(raw[:, s, :], source).then_inc(raw_in[s], 16)

            for s in range(SLOTS):
                sp.wait_ge(mod_raw_used[s], MOD_STEPS)
                load_panel("conv", s, 0, conv_panels[0, s])
            with sp.Fori(1, KB) as j:
                for s in range(4):
                    load_panel("conv", s, j, conv_panels[j, s])

            for h in range(HEADS):
                for c in range(0, GRID_W, 32):
                    src = bass.AP(tensor=rpb_padded.tensor, offset=h * REL * PADW + GRID_W - 1 - c,
                                  ap=[[PADW, REL], [-1, 32], [1, GRID_W]])
                    sp.dma_start(bias_dram[h, c:c + 32].rearrange("c r k -> r c k"), src).then_inc(bias_in, 16)

            def load_ffn0(j, slots=(0, 1, 2)):
                for s in slots:
                    load_panel("ffn0", s, j, ffn_panels[0, j, s])

            def load_rest(g, pair):
                at_least(sp, rest_acc, GROUP_STEPS * g + 4 * (pair - 1))
                sp.dma_start(mod_in[pair % 2][:], mod_rest[g, 2 * pair:2 * pair + 2].rearrange("k p c -> p k c")
                             ).then_inc(rest_in[pair % 2], 16)
            load_ffn0(0)
            load_ffn0(1)
            sp.wait_ge(hi_done[3], base["v"][3])
            sp.wait_ge(lo_done[3], base["v"][3])
            sp.wait_ge(conv.out, KB * KB * len(ALL))
            load_rest(0, 0)
            load_rest(0, 1)
            with sp.Fori(2, MOD_GROUPS + 1) as j:
                load_ffn0(j, (0, 1))
                load_rest(j - 2, 2)
                load_rest(j - 2, 3)
                load_rest(j - 1, 0)
                load_rest(j - 1, 1)
                load_ffn0(j, (2,))
            load_ffn0(MOD_GROUPS + 1, (0, 1))
            load_rest(MOD_GROUPS - 1, 2)
            load_rest(MOD_GROUPS - 1, 3)
            load_ffn0(MOD_GROUPS + 1, (2,))
            with sp.Fori(MOD_GROUPS + 2, HIDDEN) as j:
                load_ffn0(j)
            sp.wait_ge(rest_acc, GROUP_STEPS * MOD_GROUPS)

            for s in range(4):
                load_panel("v", s, 0, v_panels[s])

            def store_v(i, quarter):
                for t in range(TOK_TILES):
                    n = (2 * i + quarter) * TOK_TILES + t
                    sp.wait_ge(v_hi_done, n + 1)
                    sp.wait_ge(v_lo_done, n + 5)
                    for part, stage in enumerate((stage_v_hi, stage_v_lo)):
                        h0 = (2 * i + quarter) * 4
                        sp.dma_start(v_dram[part][h0:h0 + 4, t].rearrange("h p d -> p h d"),
                                     stage[:, t % 2].rearrange("p (h d) -> p h d", d=DH)).then_inc(v_out[t % 2], 16)
                    if t == TOK_TILES // 2 + 1:
                        for s in (0, 1):
                            if i == 0:
                                load_panel("v", 2 * quarter + s, 1, v_panels[4 + 2 * quarter + s])
                            elif quarter == 0:
                                load_panel("qk", s, 0, qk_panels[0, s])
            store_v(0, 0)
            store_v(0, 1)
            store_v(1, 0)
            store_v(1, 1)

            def store_qk(i):
                sp.wait_ge(q_lo_done, len(LAT) * (i + 1))
                sp.dma_start(q_dram[0][i], stage_q_hi[:]).then_inc(q_out, 16)
                sp.dma_start(q_dram[1][i], stage_q_lo[:]).then_inc(q_out, 16)
                sp.wait_ge(k_lo_done, len(ALL) * (i + 1))
                sp.dma_start(k_dram[0][i], stage_k_hi[:]).then_inc(k_out, 16)
                sp.dma_start(k_dram[1][i], stage_k_lo[:]).then_inc(k_out, 16)
            with sp.Fori(1, PAIRS) as i:
                for s in range(2):
                    load_panel("qk", s, i, qk_panels[i, s])
                store_qk(i - 1)
            store_qk(PAIRS - 1)

            sp.wait_ge(q_out, 32 * (PAIRS - 1))
            sp.wait_ge(k_out, 32 * (PAIRS - 1))
            for n in range(2):
                sp.wait_ge(v_out[n], 16 * 4 * TOK_TILES)
            sp.wait_ge(bias_in, 32 * HEADS)
            sp.wait_ge(k_ready, len(ALL) * PAIRS)

            def load_head(i, b):
                at_least(sp, s_done, 16 * i + 8 * b - 8)
                sp.dma_start(bias_full[0:GRID_W, b, 1:REL], bias_dram[2 * i + b, :, 1:REL]).then_inc(bias_rows_in[b], 16)
                sp.dma_start(bias_full[GRID_W:P, b, 1:REL], bias_dram[2 * i + b, :, 0:REL - 1]).then_inc(bias_rows_in[b], 16)
                for part in range(2):
                    sp.dma_start(q_st[part * DH:(part + 1) * DH, b].bitcast(F32),
                                 q_dram[part][i, b * DH:(b + 1) * DH, :]).then_inc(qk_in[b], 16)
                for part, dst in enumerate((k_hi, k_lo)):
                    for half in range(2):
                        sp.dma_start(dst[half * DH:(half + 1) * DH, b].bitcast(F32),
                                     k_dram[part][i, b * DH:(b + 1) * DH, :]).then_inc(qk_in[b], 16)
                at_least(sp, pv_ready, 8 * i + 4 * b - 4)
                for part in range(2):
                    sp.dma_start(v_st[:, b, :, part * DH:(part + 1) * DH].bitcast(F32),
                                 v_dram[part][2 * i + b].rearrange("t p d -> p t d")).then_inc(v_in[b], 16)
            load_head(0, 0)
            load_head(0, 1)
            sp.wait_ge(q_out, 32 * PAIRS)
            sp.wait_ge(k_out, 32 * PAIRS)
            with sp.Fori(1, PAIRS) as i:
                load_head(i, 0)
                load_head(i, 1)

            sp.wait_ge(s_ready, 2 * UNITS * PAIRS)
            sp.wait_ge(pv_ready, UNITS * PAIRS - UNITS // 2)
            for p in range(PAIRS):
                load_panel("wo", p % 4, p // 4, wo_panels[p])
            with sp.Fori(0, HIDDEN) as j:
                for s in range(3):
                    load_panel("ffn1", s, j, ffn_panels[1, j, s])
            for b, (t0, tn) in enumerate(LAT):
                for kb in range(KB):
                    sp.wait_ge(final_done, b * KB + kb + 1)
                    sp.dma_start(out_t[kb, :, t0:t0 + tn], residual[:, kb, t0:t0 + tn]).then_inc(final_out, 16)
            sp.wait_ge(final_out, 16 * KB * len(LAT))

        @block.tensor
        def _(pe):
            def mod_rows_of(i, b):
                at_least(pe, mod_copied, i - 1)
                for s in range(SLOTS):
                    pe.wait_ge(mod_raw_in[s], (i + 1) * 16)
                    for kb in range(KB):
                        mm = pe.matmul(psum[0:2, b, s * P:(s + 1) * P], silu_c[:, kb, :],
                                       raw[:, s, kb * P:(kb + 1) * P], start=(kb == 0), stop=(kb == KB - 1))
                    mm.then_inc(mod_raw_used[s], 1)

            def mod_turn(i, b):
                pe.wait_ge(mod_copied, i + 1)
                at_least(pe, mod_ready, i - 1)
                pe.sem_inc(pe_passed, 1)
                for s in range(SLOTS):
                    mm = pe.transpose(psum[:, 6 + b, 2 * s:2 * s + 2], mod_rows[0:2, b, s * P:(s + 1) * P],
                                      ident[0:2, 0:2])
                mm.then_inc(mod_turned, 1)

            def norm_sum(n, tiles, b, kb):
                q = b * KB + kb
                pe.wait_ge(norms[n].squared, q + 1)
                pe.matmul(psum[:, 3 + b, 0:tiles[b][1]], ones[:], squares[:, q % 2, 0:tiles[b][1]],
                          start=(kb == 0), stop=(kb == KB - 1)).then_inc(norms[n].summed, 1)

            def norm_sums(n, tiles, b):
                for kb in range(KB):
                    norm_sum(n, tiles, b, kb)

            pe.wait_ge(silu_done, 1)
            pe.wait_ge(consts, CONSTS)
            mod_rows_of(0, 0)
            mod_rows_of(1, 1)
            mod_turn(0, 0)

            def mod_pair(i):
                mod_rows_of(2 * i, 0)
                mod_turn(2 * i - 1, 1)
                mod_rows_of(2 * i + 1, 1)
                mod_turn(2 * i, 0)
            with pe.Fori(1, MOD_HALF) as i:
                mod_pair(i)
            for b in range(len(ALL)):
                norm_sums(0, ALL, b)
            with pe.Fori(MOD_HALF, MOD_STEPS // 2) as i:
                mod_pair(i)
            mod_turn(MOD_STEPS - 1, 1)
            pe.wait_ge(mod_ready, MOD_STEPS)

            def project(phase, s, i, bank, tiles, ready, extra=lambda kb: None, acts=(act_hi, act_lo)):
                pe.wait_ge(lo_done[s], base[phase][s] + i + 1)
                for kb in range(KB):
                    for n, (w, h) in enumerate(((w_hi, 0), (w_hi, 1), (w_lo, 0))):
                        for b, (t0, tn) in enumerate(tiles):
                            mm = pe.matmul(psum[:, bank + b, 0:tn], w[:, s, kb, :], acts[h][:, kb, t0:t0 + tn],
                                           start=(kb == 0 and n == 0), stop=(kb == KB - 1 and n == 2))
                            if kb == KB - 1 and n == 2:
                                mm.then_inc(ready, 1)
                    extra(kb)

            def project_behind_norm(n, phase, slots, banks, tiles, readies):
                for b, (t0, tn) in enumerate(tiles):
                    for kb in range(KB):
                        wait_lows(pe, norms[n], b * KB + kb)
                        for s, bank, ready in zip(slots, banks, readies):
                            if b == kb == 0:
                                pe.wait_ge(lo_done[s], base[phase][s] + 1)
                            for part, (w, h) in enumerate(((w_hi, act_hi), (w_hi, act_lo), (w_lo, act_hi))):
                                mm = pe.matmul(psum[:, bank + b, 0:tn], w[:, s, kb, :], h[:, kb, t0:t0 + tn],
                                               start=(kb == 0 and part == 0), stop=(kb == KB - 1 and part == 2))
                            if kb == KB - 1:
                                mm.then_inc(ready, 1)
                        if n in (1, 2) and b + 1 < len(tiles) and kb < KB // 2:
                            norm_sum(n, tiles, b + 1, 2 * kb)
                            norm_sum(n, tiles, b + 1, 2 * kb + 1)

            def out_piece(m, s, ob, r, j, count, t0, tn):
                pe.wait_ge(m.added, j * count + r + 1)
                for n, (w, h) in enumerate(((w_hi, prod_hi), (w_hi, prod_lo), (w_lo, prod_hi))):
                    mm = pe.matmul(psum[:, 6 + r % 2, 0:tn], w[:, s, ob, :], h[:, t0:t0 + tn],
                                   start=(n == 0), stop=(n == 2))
                mm.then_inc(m.out, 1)

            def out_pieces(m, phase, s, j, tiles, pieces):
                for r in pieces:
                    if r == 0:
                        pe.wait_ge(lo_done[s], base[phase][s] + j + 1)
                        pe.wait_ge(m.lo, len(tiles) * (j + 1))
                    ob, b = divmod(r, len(tiles))
                    out_piece(m, s, ob, r, j, KB * len(tiles), *tiles[b])

            def out_last(m, phase, s, j, tiles, n):
                pe.wait_ge(lo_done[s], base[phase][s] + j + 1)
                for b, (t0, tn) in enumerate(tiles):
                    pe.wait_ge(m.lo, len(tiles) * j + b + 1)
                    for ob in range(KB):
                        out_piece(m, s, ob, b * KB + ob, j, KB * len(tiles), t0, tn)
                        if b == len(tiles) - 1 and ob == KB // 2:
                            norm_sums(n, tiles, 0)

            def spread(counts):
                return [range(sum(counts[:kb]), sum(counts[:kb + 1])) for kb in range(len(counts))]

            conv_spread = spread([0] * 4 + [1] * 4 + [1] * 8 + [0] * 3 + [2, 2, 3, 3, 2])

            def conv_step(j):
                def between(projection):
                    return lambda kb: out_pieces(conv, "conv", 3, j - 1, ALL, conv_spread[projection * KB + kb])

                prev = not (isinstance(j, int) and j == 0)
                if prev:
                    at_least(pe, conv.c_copied, len(ALL) * j)
                    project("conv", 0, j, 0, ALL, conv.a, between(0))
                    pe.wait_ge(conv.b_used, len(ALL) * j)
                    project("conv", 1, j, 3, ALL, conv.b, between(1))
                    pe.wait_ge(conv.a_copied, len(ALL) * (j + 1))
                    project("conv", 2, j, 0, ALL, conv.c, between(2))
                else:
                    project_behind_norm(0, "conv", (0, 1), (0, 3), ALL, (conv.a, conv.b))
                    pe.wait_ge(conv.a_copied, len(ALL))
                    project("conv", 2, j, 0, ALL, conv.c)
            conv_step(0)
            with pe.Fori(1, KB) as j:
                conv_step(j)
            out_last(conv, "conv", 3, KB - 1, ALL, 1)

            def rest_sums(g):
                pe.wait_ge(rest_acc, GROUP_STEPS * (g + 1))
                for c in range(2):
                    for block in range(GROUP_BLOCKS):
                        at = BANK // 2 + c * GROUP_BLOCKS + block
                        mm = pe.matmul(psum[:, 5, at:at + 1], mod_acc[:, c, block * P:(block + 1) * P],
                                       ones[:, 0:1], start=True, stop=True)
                mm.then_inc(rest_summed, 1)

            def ffn_step(m, phase, n, tiles, j, summed=None):
                if isinstance(j, int) and j == 0:
                    project_behind_norm(n, phase, (0, 1), (0, 3), tiles, (m.a, m.b))
                    return
                pe.wait_ge(m.a_copied, len(tiles) * j)

                pieces = spread([0] * 4 + [2] * 12 if len(tiles) == 3 else [0] * 4 + [1] * 4 + [2, 1] * 4)

                def between(kb):
                    if kb == 2 and summed is not None:
                        pe.wait_ge(m.b_used, len(tiles) * j)
                        rest_sums(summed)
                    out_pieces(m, phase, 2, j - 1, tiles, pieces[kb])
                project(phase, 0, j, 0, tiles, m.a, between)
                pe.wait_ge(m.b_used, len(tiles) * j)
                if summed is not None:
                    pe.wait_ge(rest_ready, 2 * summed + 2)
                project(phase, 1, j, 3, tiles, m.b,
                        lambda kb: out_pieces(m, phase, 2, j - 1, tiles, pieces[KB + kb]))

            ffn_step(ffns[0], "ffn0", 1, ALL, 0)
            ffn_step(ffns[0], "ffn0", 1, ALL, 1)
            with pe.Fori(2, MOD_GROUPS + 2) as j:
                ffn_step(ffns[0], "ffn0", 1, ALL, j, summed=j - 2)
            with pe.Fori(MOD_GROUPS + 2, HIDDEN) as j:
                ffn_step(ffns[0], "ffn0", 1, ALL, j)
            out_last(ffns[0], "ffn0", 2, HIDDEN - 1, ALL, 2)

            def v_quarter(i, quarter):
                for s in (2 * quarter, 2 * quarter + 1):
                    pe.wait_ge(lo_done[s], base["v"][s] + i + 1)
                for t in range(TOK_TILES):
                    n = (2 * i + quarter) * TOK_TILES + t
                    if n * P % BANK == 0 and n < TOK_TILES:
                        b = n * P // BANK
                        if b == 0:
                            norm_sums(2, ALL, 1)
                        wait_lows(pe, norms[2], b * KB + KB - 1)
                    pe.wait_ge(v_lo_done, n + 1)
                    for kb in range(KB):
                        for part, (h, w) in enumerate(((act_hi, w_hi), (act_lo, w_hi), (act_hi, w_lo))):
                            mm = pe.matmul(psum[:, V_BANKS[n % 4], 0:2 * P], h[:, kb, t * P:(t + 1) * P],
                                           w[:, 2 * quarter:2 * quarter + 2, kb, :],
                                           start=(kb == 0 and part == 0), stop=(kb == KB - 1 and part == 2))
                    mm.then_inc(v_ready, 1)
                    if n < 4:
                        norm_sum(2, ALL, 2, 2 * n)
                        norm_sum(2, ALL, 2, 2 * n + 1)
            for i in range(2):
                v_quarter(i, 0)
                v_quarter(i, 1)

            def qk_step(i):
                at_least(pe, q_lo_done, len(LAT) * i)
                if isinstance(i, int):
                    pe.wait_ge(v_lo_done, 4 * TOK_TILES + 4)
                project("qk", 0, i, 0, LAT, q_ready)
                at_least(pe, k_lo_done, len(ALL) * i)
                project("qk", 1, i, 3, ALL, k_ready)
            qk_step(0)
            with pe.Fori(1, PAIRS) as i:
                qk_step(i)

            def scores(i, u, ab):
                b = u // 4
                if u % 4 == 0 and ab == 0:
                    pe.wait_ge(qk_in[b], 96 * (i + 1))
                at_least(pe, s_done, 16 * i + 2 * u + ab - 1)
                q0 = (4 * (u % 4) + 2 * ab) * GRID_W
                row0, rows = unit_row(u, ab)
                k0 = row0 * GRID_W
                rest = rows * GRID_W - TC
                for bank, col, key, n in ((0, 0, TL, TC), (0, TC, k0, TC), (1, 0, k0 + TC, rest)):
                    for part, k in enumerate((k_hi, k_lo)):
                        mm = pe.matmul(psum[:, 2 * ab + bank, col:col + n], q_st[:, b, q0:q0 + P],
                                       k[:, b, key:key + n], start=(part == 0), stop=(part == 1))
                mm.then_inc(s_ready, 1)

            def turn(i, u, g):
                n = PAIR_GROUPS * i + group0[u] + g
                at_least(pe, pt_lo_done, n - 1)
                if g == 0:
                    pe.wait_ge(probs_done, 16 * i + 2 * u + 2)
                col = 0
                for slot, _, starts in GROUPS[u % 4][g]:
                    for ab, start in enumerate(starts):
                        if start is not None:
                            mm = pe.transpose(psum[:, 4 + (group0[u] + g) % 2, col:col + P],
                                              probs[:, 2 * (u % 2) + ab, start:start + P], ident[:])
                            col += P
                mm.then_inc(pt_ready, 1)

            def values(i, u, g):
                if g == 0:
                    at_least(pe, sum_done, UNITS * i + u - 1)
                    if u % 4 == 0:
                        pe.wait_ge(v_in[u // 4], 32 * (i + 1))
                pe.wait_ge(pt_lo_done, PAIR_GROUPS * i + group0[u] + g + 1)
                groups = GROUPS[u % 4]
                tile0 = ROW0[u % 4][0] * GRID_W // P
                for m, (slot, key, _) in enumerate(groups[g]):
                    tile = {"c0": TL // P, "c1": TL // P + 1}.get(key, tile0 + key if isinstance(key, int) else 0)
                    for part, pt in enumerate((pt_hi, pt_lo)):
                        mm = pe.matmul(psum[:, 6 + u % 2, 0:2 * P], v_st[:, u // 4, tile, :], pt[:, slot, :],
                                       start=(g == 0 and m == 0 and part == 0),
                                       stop=(g == len(groups) - 1 and m == 1 and part == 1))
                if g == len(groups) - 1:
                    mm.then_inc(pv_ready, 1)

            def attention(i, last):
                for u in range(UNITS):
                    n = len(GROUPS[u % 4])
                    for g in range(n):
                        if g < 2:
                            if u + 2 < UNITS:
                                scores(i, u + 2, g)
                            elif not last:
                                scores(i + 1, u + 2 - UNITS, g)
                        if g + 2 < n:
                            turn(i, u, g + 2)
                        elif u < UNITS - 1:
                            turn(i, u + 1, g + 2 - n)
                        elif not last:
                            turn(i + 1, 0, g + 2 - n)
                        values(i, u, g)
            pe.wait_ge(q_lo_done, len(LAT) * PAIRS)
            pe.wait_ge(k_lo_done, len(ALL) * PAIRS)
            for u in range(2):
                for ab in range(2):
                    scores(0, u, ab)
            pe.wait_ge(attn_consts, 5)
            turn(0, 0, 0)
            turn(0, 0, 1)
            attention(0, False)
            with pe.Fori(1, PAIRS - 1) as i:
                attention(i, False)
            attention(PAIRS - 1, True)

            def wo_sums(kb):
                for b, (t0, tn) in enumerate(LAT):
                    q = len(LAT) * kb + b
                    pe.wait_ge(norms[3].squared, q + 1)
                    pe.matmul(psum[:, 3 + b, 0:tn], ones[:], squares[:, q % 2, 0:tn],
                              start=(kb == 0), stop=(kb == KB - 1)).then_inc(norms[3].summed, 1)

            pe.wait_ge(o_lo_done, UNITS * PAIRS)
            for p in range(PAIRS):
                at_least(pe, y_added, len(LAT) * (p - 1))
                project("wo", p % 4, p // 4, 6 * (p % 2), LAT, y_ready, acts=(o_hi, o_lo))
                if p > 0:
                    wo_sums(p - 1)
            wo_sums(PAIRS - 1)

            ffn_step(ffns[1], "ffn1", 3, LAT, 0)
            with pe.Fori(1, HIDDEN) as j:
                ffn_step(ffns[1], "ffn1", 3, LAT, j)
            out_last(ffns[1], "ffn1", 2, HIDDEN - 1, LAT, 4)
            norm_sums(4, LAT, 1)

        @block.scalar
        def _(act):
            act.wait_ge(small_in, 64)
            act.activation(silu_c[:], cond[:], ACT.Silu).then_inc(silu_done, 1)

            def split_hi(phase, s, i, waits=()):
                for semaphore, value in waits:
                    act.wait_ge(semaphore, value)
                n = base[phase][s] + i
                act.wait_ge(raw_in[s], (n + 1) * 16)
                act.activation(panel(w_hi, s), raw[:, s], ACT.Copy).then_inc(hi_done[s], 1)

            def norm_squares(n, tiles, b, blocks):
                t0, tn = tiles[b]
                for kb in blocks:
                    q = b * KB + kb
                    at_least(act, norms[n].summed, q - 1)
                    act.activation(squares[:, q % 2, 0:tn], residual[:, kb, t0:t0 + tn],
                                   ACT.Square).then_inc(norms[n].squared, 1)

            def norm_root(n, tiles, b):
                t0, tn = tiles[b]
                act.wait_ge(norms[n].summed, KB * (b + 1) if n != 3 else KB * len(tiles))
                act.activation(rstd[:, t0:t0 + tn], psum[:, 3 + b, 0:tn], ACT.Sqrt, bias=eps_col[:, 0:1],
                               scale=1.0 / D).then_inc(norms[n].rooted, 1)

            def norm(n, tiles, ready=None, after=None):
                m = norms[n]
                shift = (n // 2) * MODS + (n % 2) * 3 * KB

                if n == 2:
                    act.wait_ge(rest_ready, 2 * MOD_GROUPS)

                def high(b, kb):
                    t0, tn = tiles[b]
                    q, kind = b * KB + kb, kind_of(t0)
                    act.wait_ge(m.scaled, q + 1)
                    by = modulation[:, shift + kb, kind:kind + 1]
                    if kb in POOL_LO:
                        act.activation(centred[:, q % 2, 0:tn], centred[:, q % 2, 0:tn], ACT.Identity,
                                       bias=by).then_inc(m.shifted, 1)
                        act.wait_ge(m.shifted, pool_lows(q))
                        act.activation(act_hi[:, kb, t0:t0 + tn], centred[:, q % 2, 0:tn],
                                       ACT.Copy).then_inc(m.hi, 1)
                    else:
                        act.activation(act_hi[:, kb, t0:t0 + tn], centred[:, q % 2, 0:tn], ACT.Identity,
                                       bias=by).then_inc(m.hi, 1)

                fused = n not in (0, 3)
                if fused:
                    ready(0)
                    norm_squares(n, tiles, 0, range(KB))
                    norm_root(n, tiles, 0)
                for b in range(len(tiles)):
                    for kb in range(KB):
                        if n < 4:
                            high(b, kb)
                        if fused and b + 1 < len(tiles):
                            if kb == 0:
                                ready(b + 1)
                            if kb < KB // 2:
                                norm_squares(n, tiles, b + 1, (2 * kb, 2 * kb + 1))
                            elif kb == KB // 2:
                                norm_root(n, tiles, b + 1)
                    if after is not None:
                        after(b)

            act.wait_ge(consts, CONSTS)
            act.wait_ge(x_in, 32)
            for b in range(len(ALL)):
                norm_squares(0, ALL, b, range(KB))
                norm_root(0, ALL, b)
            for s in range(3):
                split_hi("conv", s, 0)
            act.wait_ge(mod_ready, MOD_STEPS)
            norm(0, ALL)

            def product_high(m, j, tiles, padding=False):
                at_least(act, m.out, KB * len(tiles) * j)
                for b, (t0, tn) in enumerate(tiles):
                    act.wait_ge(m.prod, len(tiles) * j + b + 1)
                    at = pad_of(t0) if padding else t0
                    act.activation(prod_hi[:, t0:t0 + tn], prod[:, at:at + tn], ACT.Copy).then_inc(m.hi, 1)

            def conv_step(j, last=False):
                n = len(ALL)
                at_least(act, conv.prod, n * j)
                for b, (t0, tn) in enumerate(ALL):
                    act.wait_ge(conv.a, n * j + b + 1)
                    act.activation(gate[:, t0:t0 + tn], psum[:, b, 0:tn], ACT.Copy).then_inc(conv.a_copied, 1)
                split_hi("conv", 0, j + 1)
                split_hi("conv", 1, j + 1, [(conv.b, n * j + n)])
                for b, (t0, tn) in enumerate(ALL):
                    act.wait_ge(conv.c, n * j + b + 1)
                    act.wait_ge(conv.b_used, n * j + b + 1)
                    act.activation(gate[:, t0:t0 + tn], psum[:, b, 0:tn], ACT.Copy).then_inc(conv.c_copied, 1)
                if not last:
                    split_hi("conv", 2, j + 1)
                at_least(act, conv.out, KB * n * j)
                split_hi("conv", 3, j)
                product_high(conv, j, ALL, padding=True)

            conv_step(0)
            with act.Fori(1, KB - 1) as j:
                conv_step(j)
            conv_step(KB - 1, last=True)

            def ffn_step(m, phase, tiles, j, last=False):
                n = len(tiles)
                at_least(act, m.prod, n * j)
                for b, (t0, tn) in enumerate(tiles):
                    act.wait_ge(m.a, n * j + b + 1)
                    act.activation(gate[:, t0:t0 + tn], psum[:, b, 0:tn], ACT.Silu).then_inc(m.a_copied, 1)
                if not last:
                    split_hi(phase, 0, j + 1)
                    split_hi(phase, 1, j + 1, [(m.b, n * j + n)])
                at_least(act, m.out, KB * n * j)
                split_hi(phase, 2, j)
                product_high(m, j, tiles)

            done = KB * len(ALL)
            norm(1, ALL, lambda b: act.wait_ge(conv.added, done * (KB - 1) + KB * (b + 1) + 2))
            ffn_step(ffns[0], "ffn0", ALL, 0)
            with act.Fori(1, HIDDEN) as j:
                ffn_step(ffns[0], "ffn0", ALL, j)

            def v_high(n):
                act.wait_ge(v_ready, n + 1)
                at_least(act, v_out[n % 2], 32 * (n // 2))
                act.activation(stage_v_hi[:, n % 2].bitcast(F32R), psum[:, V_BANKS[n % 4], 0:2 * P],
                               ACT.Copy).then_inc(v_hi_done, 1)

            def first_v(b):
                if b == 1:
                    for n in range(4):
                        v_high(n)
            norm(2, ALL, lambda b: act.wait_ge(ffns[0].added, done * (HIDDEN - 1) + KB * (b + 1) + 2), first_v)
            for quarter in range(4):
                for t in range(TOK_TILES):
                    n = quarter * TOK_TILES + t
                    if n >= 4:
                        v_high(n)
                    if t == TOK_TILES // 2 - 1:
                        for s in ((2, 3) if quarter % 2 == 0 else (0, 1)):
                            split_hi("v", s, (quarter + 1) // 2)

            def qk_step(i, last=False):
                at_least(act, q_out, 32 * i)
                for b, (t0, tn) in enumerate(LAT):
                    act.wait_ge(q_ready, len(LAT) * i + b + 1)
                    act.activation(stage_q_hi[:, t0:t0 + tn].bitcast(F32R), psum[:, b, 0:tn], ACT.Copy,
                                   scale=SCALE).then_inc(q_hi_done, 1)
                if not last:
                    split_hi("qk", 0, i + 1)
                at_least(act, k_out, 32 * i)
                for b, (t0, tn) in enumerate(ALL):
                    act.wait_ge(k_ready, len(ALL) * i + b + 1)
                    act.activation(stage_k_hi[:, t0:t0 + tn].bitcast(F32R), psum[:, 3 + b, 0:tn],
                                   ACT.Copy).then_inc(k_hi_done, 1)
                if not last:
                    split_hi("qk", 1, i + 1)
            for n in range(2):
                act.wait_ge(v_out[n], 16 * 4 * TOK_TILES)
            qk_step(0)
            with act.Fori(1, PAIRS - 1) as i:
                qk_step(i)
            qk_step(PAIRS - 1, last=True)

            def exponentials(i, u, ab):
                n = 16 * i + 2 * u + ab
                keys = TC + unit_row(u, ab)[1] * GRID_W
                pb = 2 * (u % 2) + ab
                act.wait_ge(s_done, n + 1)
                act.activation(probs[:, pb, 0:keys], neg_s[:, ab, 0:keys], ACT.Exp, bias=stats[:, pb, 1:2],
                               scale=-1.0, accum_out=stats[:, pb, 2:3]).then_inc(exp_done, 1)

            def pt_high(i, u, g):
                act.wait_ge(pt_ready, PAIR_GROUPS * i + group0[u] + g + 1)
                dst, n = pt_target(pt_hi, GROUPS[u % 4][g])
                src = psum[:, 4 + (group0[u] + g) % 2, 0:n]
                if n == 4 * P:
                    src = src.rearrange("p (s q) -> p s q", s=2)
                act.activation(dst, src, ACT.Copy).then_inc(pt_hi_done, 1)

            def half(i, u):
                act.wait_ge(pv_ready, UNITS * i + u + 1)
                at_least(act, sum_done, UNITS * i + u)
                act.activation(o_half[0:DH, :], psum[DH:P, 6 + u % 2, 0:2 * P], ACT.Copy).then_inc(half_done, 1)

            def out_high(i, u):
                h0, q0 = DH * (u // 4), 4 * (u % 4) * GRID_W
                act.wait_ge(sum_done, UNITS * i + u + 1)
                act.activation(o_hi[h0:h0 + DH, i, q0:q0 + 2 * P], o_sum[h0:h0 + DH, :], ACT.Copy).then_inc(o_hi_done, 1)

            def attention(i, last):
                first = isinstance(i, int) and i == 0
                for u in range(UNITS):
                    nxt_i, nxt_u = (i, u + 1) if u < UNITS - 1 else (i + 1, 0)
                    more = not (last and u == UNITS - 1)
                    if more:
                        exponentials(nxt_i, nxt_u, 0)
                    pt_high(i, u, 0)
                    if more:
                        exponentials(nxt_i, nxt_u, 1)
                    pt_high(i, u, 1)
                    if not (first and u == 0):
                        half(*before(i, u))
                    pt_high(i, u, 2)
                    if not (first and u == 0):
                        out_high(*before(i, u))
                    if len(GROUPS[u % 4]) == 4:
                        pt_high(i, u, 3)
            act.wait_ge(attn_consts, 5)
            act.wait_ge(qk_in[0], 96)
            exponentials(0, 0, 0)
            exponentials(0, 0, 1)
            attention(0, False)
            with act.Fori(1, PAIRS - 1) as i:
                attention(i, False)
            attention(PAIRS - 1, True)
            half(PAIRS - 1, UNITS - 1)
            out_high(PAIRS - 1, UNITS - 1)

            for s in range(4):
                split_hi("wo", s, 0)
            for p in range(PAIRS):
                if p < PAIRS - 2:
                    split_hi("wo", p % 4, p // 4 + 1, [(y_ready, len(LAT) * (p + 1))])
                for b, (t0, tn) in enumerate(LAT):
                    q = len(LAT) * p + b
                    act.wait_ge(y_added, q + 1)
                    at_least(act, norms[3].summed, q - 1)
                    act.activation(squares[:, q % 2, 0:tn], residual[:, p, t0:t0 + tn],
                                   ACT.Square).then_inc(norms[3].squared, 1)
            for b in range(len(LAT)):
                norm_root(3, LAT, b)
            norm(3, LAT)
            ffn_step(ffns[1], "ffn1", LAT, 0)
            with act.Fori(1, HIDDEN - 1) as j:
                ffn_step(ffns[1], "ffn1", LAT, j)
            ffn_step(ffns[1], "ffn1", LAT, HIDDEN - 1, last=True)
            done_lat = KB * len(LAT)
            norm(4, LAT, lambda b: act.wait_ge(ffns[1].added, done_lat * (HIDDEN - 1) + KB * (b + 1) + 2))

        @block.vector
        def _(dve):
            dve.memset(eps_col[:], EPS).then_inc(consts, 1)
            dve.memset(zeros[:], 0.0).then_inc(attn_consts, 1)
            dve.memset(stats[:], 0.0).then_inc(attn_consts, 1)
            dve.wait_ge(small_in, 64)

            def mod_copy(i, b):
                at_least(dve, mod_turned, i - 1)
                dve.wait_ge(mod_raw_used[SLOTS - 1], i + 1)
                dve.tensor_copy(mod_rows[:, b, :], psum[0:2, b, :]).then_inc(mod_copied, 1)

            def mod_column(i, b):
                dve.wait_ge(mod_turned, i + 1)
                bias = mod_bias_sb[:, bass.ds(i * SLOTS, SLOTS)]
                for c in range(2):
                    ins = dve.tensor_tensor(modulation[:, bass.ds(i * SLOTS, SLOTS), c],
                                            psum[:, 6 + b, c:2 * SLOTS:2], bias, ALU.add)
                ins.then_inc(mod_ready, 1)

            mod_copy(0, 0)
            mod_copy(1, 1)
            mod_column(0, 0)

            def mod_pair(i):
                mod_copy(2 * i, 0)
                mod_column(2 * i - 1, 1)
                mod_copy(2 * i + 1, 1)
                mod_column(2 * i, 0)

            def norm_invert(n, tiles, b, quarters):
                t0, tn = tiles[b]
                dve.wait_ge(norms[n].rooted, b + 1)
                for quarter in quarters:
                    part = rstd[:, t0 + quarter * tn // 4:t0 + (quarter + 1) * tn // 4]
                    dve.reciprocal(part, part).then_inc(norms[n].inverted, 1)
            with dve.Fori(1, MOD_HALF) as i:
                mod_pair(i)
            for b in range(len(ALL)):
                norm_invert(0, ALL, b, range(4))
            with dve.Fori(MOD_HALF, MOD_STEPS // 2) as i:
                mod_pair(i)
            mod_column(MOD_STEPS - 1, 1)
            dve.wait_ge(mod_ready, MOD_STEPS)

            def norm_scales(layer):
                for n in (2 * layer, 2 * layer + 1):
                    first = (n // 2) * MODS + (n % 2) * 3 * KB
                    for c in range(2):
                        dve.scalar_tensor_tensor(out=norm_scale[:, n, :, c],
                                                 in0=modulation[:, first + KB:first + 2 * KB, c],
                                                 scalar=1.0, in1=gains[:, n, :], op0=ALU.add,
                                                 op1=ALU.mult).then_inc(scales_done, 1)
                dve.wait_ge(scales_done, 4 * layer + 4)
            norm_scales(0)

            def norm(n, tiles, after=None):
                m = norms[n]
                shift = (n // 2) * MODS + (n % 2) * 3 * KB

                def low(b, kb):
                    t0, tn = tiles[b]
                    q, kind = b * KB + kb, kind_of(t0)
                    dve.wait_ge(m.hi, q + 1)
                    dve.scalar_tensor_tensor(out=act_lo[:, kb, t0:t0 + tn], in0=centred[:, q % 2, 0:tn],
                                             scalar=modulation[:, shift + kb, kind:kind + 1],
                                             in1=act_hi[:, kb, t0:t0 + tn], op0=ALU.add,
                                             op1=ALU.subtract).then_inc(m.lo_dve, 1)

                if n > 0:
                    norm_invert(n, tiles, 0, range(4))
                for b, (t0, tn) in enumerate(tiles):
                    kind = kind_of(t0)
                    dve.wait_ge(m.inverted, 4 * (b + 1))
                    for kb in range(KB):
                        q = b * KB + kb
                        if q > 1:
                            dve.wait_ge(m.hi, q - 1)
                            wait_lows(dve, m, q - 2)
                        dve.scalar_tensor_tensor(out=centred[:, q % 2, 0:tn], in0=residual[:, kb, t0:t0 + tn],
                                                 scalar=norm_scale[:, n, kb, kind:kind + 1],
                                                 in1=rstd[:, t0:t0 + tn], op0=ALU.mult,
                                                 op1=ALU.mult).then_inc(m.scaled, 1)
                        if kb > 0 and kb - 1 not in POOL_LO:
                            low(b, kb - 1)
                        if n > 0 and b + 1 < len(tiles) and kb in (5, 6):
                            norm_invert(n, tiles, b + 1, (kb - 5,))
                    low(b, KB - 1)
                    if n > 0 and b + 1 < len(tiles):
                        norm_invert(n, tiles, b + 1, (2, 3))
                    if after is not None:
                        after(b)
                dve.wait_ge(m.hi, KB * len(tiles))
                wait_lows(dve, m, KB * len(tiles) - 1)

            def add_piece(m, ob, r, j, count, t0, tn, gates):
                dve.wait_ge(m.out, j * count + r + 1)
                dve.scalar_tensor_tensor(out=residual[:, ob, t0:t0 + tn], in0=psum[:, 6 + r % 2, 0:tn],
                                         scalar=modulation[:, gates + ob, kind_of(t0):kind_of(t0) + 1],
                                         in1=residual[:, ob, t0:t0 + tn],
                                         op0=ALU.mult, op1=ALU.add).then_inc(m.added, 1)

            def add_block(m, ob, j, tiles, gates):
                for b, (t0, tn) in enumerate(tiles):
                    add_piece(m, ob, ob * len(tiles) + b, j, KB * len(tiles), t0, tn, gates)

            def add_last(m, j, tiles, gates):
                dve.wait_ge(m.added, j * KB * len(tiles) + 2)
                for b, (t0, tn) in enumerate(tiles):
                    for ob in range(KB):
                        add_piece(m, ob, b * KB + ob, j, KB * len(tiles), t0, tn, gates)

            def product_low(m, j, tiles, padding=False):
                for b, (t0, tn) in enumerate(tiles):
                    dve.wait_ge(m.hi, len(tiles) * j + b + 1)
                    at = pad_of(t0) if padding else t0
                    dve.tensor_tensor(prod_lo[:, t0:t0 + tn], prod[:, at:at + tn], prod_hi[:, t0:t0 + tn],
                                      ALU.subtract).then_inc(m.lo, 1)

            for n, m in enumerate((conv, *ffns)):
                dve.memset(credit[:, n:n + 1], 0.0).then_inc(m.added, 2)
            dve.memset(credit[:, 3:4], 0.0).then_inc(v_lo_done, 4)
            norm(0, ALL)
            dve.wait_ge(norms[0].summed, KB * len(ALL))
            dve.memset(padded[:], 0.0).then_inc(pads_zeroed, 1)
            dve.wait_ge(pads_zeroed, 1)

            def conv_step(j):
                n, gates = len(ALL), 2 * KB
                some = not isinstance(j, int)
                if some:
                    for ob in range(4):
                        add_block(conv, ob, j - 1, ALL, gates)
                for b, (t0, tn) in enumerate(ALL):
                    dve.wait_ge(conv.a_copied, n * j + b + 1)
                    dve.wait_ge(conv.b, n * j + b + 1)
                    at = pad_of(t0)
                    dve.tensor_tensor(padded[:, at:at + tn], psum[:, 3 + b, 0:tn], gate[:, t0:t0 + tn],
                                      ALU.mult).then_inc(conv.b_used, 1)
                dve.wait_ge(conv.b_used, n * j + n)
                at_least(dve, conv.hi, n * j)
                at_least(dve, conv.lo, n * j)
                inside = slice(1, T + 3)
                dve.tensor_scalar(prod[:, inside], padded[:, inside], taps[:, 1, bass.ds(j, 1)], None,
                                  ALU.mult).then_inc(conv.tapped, 1)
                dve.wait_ge(conv.tapped, 3 * j + 1)
                for shift, tap in ((0, 0), (2, 2)):
                    dve.scalar_tensor_tensor(out=prod[:, inside], in0=padded[:, shift:shift + T + 2],
                                             scalar=taps[:, tap, bass.ds(j, 1)], in1=prod[:, inside],
                                             op0=ALU.mult, op1=ALU.add).then_inc(conv.tapped, 1)
                    dve.wait_ge(conv.tapped, 3 * j + 2 + tap // 2)
                if some:
                    for ob in range(4, KB):
                        add_block(conv, ob, j - 1, ALL, gates)
                for b, (t0, tn) in enumerate(ALL):
                    at = pad_of(t0)
                    dve.wait_ge(conv.c_copied, n * j + b + 1)
                    dve.tensor_tensor(prod[:, at:at + tn], prod[:, at:at + tn], gate[:, t0:t0 + tn],
                                      ALU.mult).then_inc(conv.prod, 1)
                product_low(conv, j, ALL, padding=True)

            conv_step(0)
            with dve.Fori(1, KB) as j:
                conv_step(j)
            add_last(conv, KB - 1, ALL, 2 * KB)

            def rest_columns(g):
                dve.wait_ge(rest_summed, g + 1)
                cols = bass.ds(MODS + g * GROUP_BLOCKS, GROUP_BLOCKS)
                for c in range(2):
                    at = BANK // 2 + c * GROUP_BLOCKS
                    dve.tensor_tensor(modulation[:, cols, c], psum[:, 5, at:at + GROUP_BLOCKS],
                                      mod_bias_sb[:, cols], ALU.add).then_inc(rest_ready, 1)

            def rest_block(g, kb):
                if kb % 2 == 0:
                    pair = kb // 2
                    dve.wait_ge(rest_in[pair % 2], 16 * (2 * g + pair // 2 + 1))
                for c in range(2):
                    done = GROUP_STEPS * g + 2 * kb + c
                    rows, by = mod_in[kb // 2 % 2][:, kb % 2, :], silu_c[:, kb, c:c + 1]
                    if kb == 0:
                        dve.tensor_scalar(mod_acc[:, c, :], rows, by, None, ALU.mult).then_inc(rest_acc, 1)
                    else:
                        dve.wait_ge(rest_acc, done - 1)
                        dve.scalar_tensor_tensor(out=mod_acc[:, c, :], in0=rows, scalar=by, in1=mod_acc[:, c, :],
                                                 op0=ALU.mult, op1=ALU.add).then_inc(rest_acc, 1)

            def ffn_step(m, tiles, j, gates, summed=None, group=None):
                n = len(tiles)
                if summed is not None:
                    rest_columns(summed)
                if not (isinstance(j, int) and j == 0):
                    for ob in range(KB):
                        add_block(m, ob, j - 1, tiles, gates)
                        if group is not None:
                            rest_block(group, ob)
                at_least(dve, m.hi, n * j)
                at_least(dve, m.lo, n * j)
                for b, (t0, tn) in enumerate(tiles):
                    dve.wait_ge(m.a_copied, n * j + b + 1)
                    dve.wait_ge(m.b, n * j + b + 1)
                    dve.tensor_tensor(prod[:, t0:t0 + tn], psum[:, 3 + b, 0:tn], gate[:, t0:t0 + tn],
                                      ALU.mult).then_inc(m.prod, 1)
                product_low(m, j, tiles)

            norm(1, ALL)
            ffn_step(ffns[0], ALL, 0, 5 * KB)
            ffn_step(ffns[0], ALL, 1, 5 * KB, group=0)
            with dve.Fori(2, MOD_GROUPS + 1) as j:
                ffn_step(ffns[0], ALL, j, 5 * KB, summed=j - 2, group=j - 1)
            ffn_step(ffns[0], ALL, MOD_GROUPS + 1, 5 * KB, summed=MOD_GROUPS - 1)
            with dve.Fori(MOD_GROUPS + 2, HIDDEN) as j:
                ffn_step(ffns[0], ALL, j, 5 * KB)
            add_last(ffns[0], HIDDEN - 1, ALL, 5 * KB)

            dve.wait_ge(rest_ready, 2 * MOD_GROUPS)
            norm_scales(1)

            def v_low(n):
                at_least(dve, v_out[n % 2], 32 * (n // 2))
                dve.wait_ge(v_hi_done, n + 1)
                dve.tensor_tensor(stage_v_lo[:, n % 2].bitcast(F32R), psum[:, V_BANKS[n % 4], 0:2 * P],
                                  stage_v_hi[:, n % 2], ALU.subtract).then_inc(v_lo_done, 1)

            def first_v(b):
                if b == 1:
                    for n in range(4):
                        v_low(n)
            norm(2, ALL, first_v)
            for n in range(4, 4 * TOK_TILES):
                v_low(n)

            def qk_step(i):
                at_least(dve, q_out, 32 * i)
                for b, (t0, tn) in enumerate(LAT):
                    dve.wait_ge(q_hi_done, len(LAT) * i + b + 1)
                    dve.scalar_tensor_tensor(out=stage_q_lo[:, t0:t0 + tn].bitcast(F32R), in0=psum[:, b, 0:tn],
                                             scalar=SCALE, in1=stage_q_hi[:, t0:t0 + tn], op0=ALU.mult,
                                             op1=ALU.subtract).then_inc(q_lo_done, 1)
                at_least(dve, k_out, 32 * i)
                for b, (t0, tn) in enumerate(ALL):
                    dve.wait_ge(k_hi_done, len(ALL) * i + b + 1)
                    dve.tensor_tensor(stage_k_lo[:, t0:t0 + tn].bitcast(F32R), psum[:, 3 + b, 0:tn],
                                      stage_k_hi[:, t0:t0 + tn], ALU.subtract).then_inc(k_lo_done, 1)
            for n in range(2):
                dve.wait_ge(v_out[n], 16 * 4 * TOK_TILES)
            qk_step(0)
            with dve.Fori(1, PAIRS) as i:
                qk_step(i)

            dve.wait_ge(q_out, 32 * PAIRS)
            dve.wait_ge(k_out, 32 * PAIRS)
            dve.wait_ge(k_ready, len(ALL) * PAIRS)
            dve.memset(probs[:, :, KEYS_IN:], 0.0).then_inc(attn_consts, 1)
            dve.memset(pt_hi[:, 5:7, :].bitcast(F32), 0.0).then_inc(attn_consts, 1)
            dve.memset(pt_lo[:, 5:7, :].bitcast(F32), 0.0).then_inc(attn_consts, 1)
            dve.wait_ge(attn_consts, 5)

            def bias_scores(i, u, ab):
                n = 16 * i + 2 * u + ab
                b, pb = u // 4, 2 * (u % 2) + ab
                row0, rows = unit_row(u, ab)
                if ab == 0 and u % 4 == 0:
                    dve.wait_ge(bias_done, 2 * i + b + 1)
                if rows > WIN_ROWS:
                    table = bias_inner[:, b]
                else:
                    e0 = row0 - (4 * (u % 4) + 2 * ab) + WIN_ROWS - 1
                    table = bias_full[:, b, e0:e0 + rows]
                band = rows * GRID_W
                both = psum[:, 2 * ab:2 * ab + 2, :].rearrange("p b n -> p (b n)")
                dve.wait_ge(s_ready, n + 1)
                at_least(dve, exp_done, n - 1)
                dve.sem_inc(dve_passed, 1)
                dve.tensor_tensor_reduce(neg_s[:, ab, TC:TC + band], both[:, TC:TC + band],
                                         table.rearrange("p r c -> p (r c)"), -1.0, 3e38, ALU.add, ALU.min,
                                         stats[:, pb, 0:1]).then_inc(band_done, 1)
                dve.wait_ge(band_done, n + 1)
                dve.sem_inc(dve_passed, 1)
                dve.tensor_tensor_reduce(neg_s[:, ab, 0:TC], both[:, 0:TC], zeros[:], -1.0, stats[:, pb, 0:1],
                                         ALU.add, ALU.min, stats[:, pb, 1:2]).then_inc(s_done, 1)

            def invert(i, u, ab):
                n, pb = 16 * i + 2 * u + ab, 2 * (u % 2) + ab
                dve.wait_ge(exp_done, n + 1)
                dve.reciprocal(stats[:, pb, 3:4], stats[:, pb, 2:3]).then_inc(inv_done, 1)

            def pt_low(i, u, g):
                dst, n = pt_target(pt_lo, GROUPS[u % 4][g])
                hi, _ = pt_target(pt_hi, GROUPS[u % 4][g])
                src = psum[:, 4 + (group0[u] + g) % 2, 0:n]
                if n == 4 * P:
                    src = src.rearrange("p (s q) -> p s q", s=2)
                dve.wait_ge(pt_hi_done, PAIR_GROUPS * i + group0[u] + g + 1)
                dve.tensor_tensor(dst, src, hi, ALU.subtract).then_inc(pt_lo_done, 1)

            def head_sum(i, u):
                n = UNITS * i + u
                h0 = DH * (u // 4)
                dve.wait_ge(half_done, n + 1)
                at_least(dve, o_hi_done, n)
                at_least(dve, o_lo_done, n)
                dve.tensor_tensor(o_sum[h0:h0 + DH, :], psum[0:DH, 6 + u % 2, 0:2 * P], o_half[0:DH, :],
                                  ALU.add).then_inc(sum_done, 1)

            def attention(i, last):
                first = isinstance(i, int) and i == 0
                for u in range(UNITS):
                    nxt_i, nxt_u = (i, u + 1) if u < UNITS - 1 else (i + 1, 0)
                    far_i, far_u = (i, u + 2) if u + 2 < UNITS else (i + 1, u + 2 - UNITS)
                    pt_low(i, u, 0)
                    if not (last and u == UNITS - 1):
                        invert(nxt_i, nxt_u, 0)
                    pt_low(i, u, 1)
                    if not (last and u == UNITS - 1):
                        invert(nxt_i, nxt_u, 1)
                    if not (first and u == 0):
                        head_sum(*before(i, u))
                    if not (last and far_u < 2):
                        bias_scores(far_i, far_u, 0)
                    pt_low(i, u, 2)
                    if not (last and far_u < 2):
                        bias_scores(far_i, far_u, 1)
                    if len(GROUPS[u % 4]) == 4:
                        pt_low(i, u, 3)
            bias_scores(0, 0, 0)
            bias_scores(0, 0, 1)
            invert(0, 0, 0)
            bias_scores(0, 1, 0)
            invert(0, 0, 1)
            bias_scores(0, 1, 1)
            attention(0, False)
            with dve.Fori(1, PAIRS - 1) as i:
                attention(i, False)
            attention(PAIRS - 1, True)
            head_sum(PAIRS - 1, UNITS - 1)

            for p in range(PAIRS):
                for b, (t0, tn) in enumerate(LAT):
                    dve.wait_ge(y_ready, len(LAT) * p + b + 1)
                    dve.scalar_tensor_tensor(out=residual[:, p, t0:t0 + tn], in0=psum[:, 6 * (p % 2) + b, 0:tn],
                                             scalar=modulation[:, MODS + 2 * KB + p, 0:1],
                                             in1=residual[:, p, t0:t0 + tn], op0=ALU.mult,
                                             op1=ALU.add).then_inc(y_added, 1)

            norm(3, LAT)
            gates = MODS + 5 * KB
            ffn_step(ffns[1], LAT, 0, gates)
            with dve.Fori(1, HIDDEN) as j:
                ffn_step(ffns[1], LAT, j, gates)
            add_last(ffns[1], HIDDEN - 1, LAT, gates)

            for b, (t0, tn) in enumerate(LAT):
                m = norms[4]
                dve.wait_ge(m.rooted, b + 1)
                dve.reciprocal(rstd[:, t0:t0 + tn], rstd[:, t0:t0 + tn]).then_inc(m.inverted, 1)
                dve.wait_ge(m.inverted, b + 1)
                for kb in range(KB):
                    dve.scalar_tensor_tensor(out=residual[:, kb, t0:t0 + tn], in0=residual[:, kb, t0:t0 + tn],
                                             scalar=gains[:, 4, kb:kb + 1], in1=rstd[:, t0:t0 + tn],
                                             op0=ALU.mult, op1=ALU.mult).then_inc(final_done, 1)

        @block.gpsimd
        def _(pool):
            pool.memset(ident[:], 0.0).then_inc(pool_step, 1)
            pool.memset(col_mask[:], 0.0).then_inc(pool_step, 1)
            pool.memset(row_mask[:], 0.0).then_inc(pool_step, 1)
            pool.memset(ones[:], 1.0).then_inc(consts, 1)
            pool.wait_ge(pool_step, 3)
            pool.affine_select(out=ident[:], in_=ident[:], compare_op=ALU.not_equal, fill=1.0, base=0,
                               pattern=[[-1, P]], channel_multiplier=1).then_inc(consts, 1)
            reach = WIN_COLS // 2
            for half in range(2):
                h = slice(half * GRID_W, (half + 1) * GRID_W)
                left = col_mask[h, 0:GRID_W - WIN_COLS]
                pool.affine_select(out=left, in_=left, compare_op=ALU.is_ge, fill=MASKED, base=reach,
                                   pattern=[[1, GRID_W - WIN_COLS]], channel_multiplier=-1).then_inc(pool_step, 1)
                pool.wait_ge(pool_step, 4 + half)
                right = col_mask[h, WIN_COLS:GRID_W]
                pool.affine_select(out=right, in_=right, compare_op=ALU.is_ge, fill=MASKED,
                                   base=reach - 1 - WIN_COLS, pattern=[[-1, GRID_W - WIN_COLS]],
                                   channel_multiplier=1).then_inc(consts, 1)
            pool.memset(row_mask[0:GRID_W, WIN_ROWS, :], MASKED).then_inc(consts, 1)
            pool.memset(row_mask[GRID_W:P, 0, :], MASKED).then_inc(consts, 1)
            pool.wait_ge(consts, CONSTS)

            def split_lo(phase, s, i):
                pool.wait_ge(hi_done[s], base[phase][s] + i + 1)
                pool.tensor_tensor(panel(w_lo, s), raw[:, s], panel(w_hi, s), ALU.subtract).then_inc(lo_done[s], 1)

            def norm(n, tiles):
                m = norms[n]
                for b, (t0, tn) in enumerate(tiles):
                    for kb in POOL_LO:
                        q = b * KB + kb
                        pool.wait_ge(m.hi, q + 1)
                        pool.tensor_tensor(act_lo[:, kb, t0:t0 + tn], centred[:, q % 2, 0:tn],
                                           act_hi[:, kb, t0:t0 + tn], ALU.subtract).then_inc(m.lo_pool, 1)

            for s in range(3):
                split_lo("conv", s, 0)
            norm(0, ALL)

            def conv_step(j, last=False):
                for s in (0, 1) if last else (0, 1, 2):
                    split_lo("conv", s, j + 1)
                split_lo("conv", 3, j)
            conv_step(0)
            with pool.Fori(1, KB - 1) as j:
                conv_step(j)
            conv_step(KB - 1, last=True)

            def ffn_step(phase, j, last=False):
                for s in () if last else (0, 1):
                    split_lo(phase, s, j + 1)
                split_lo(phase, 2, j)
            norm(1, ALL)
            with pool.Fori(0, HIDDEN) as j:
                ffn_step("ffn0", j)
            norm(2, ALL)
            for quarter in range(4):
                for s in ((2, 3) if quarter % 2 == 0 else (0, 1)):
                    split_lo("v", s, (quarter + 1) // 2)
            with pool.Fori(0, PAIRS - 1) as i:
                for s in range(2):
                    split_lo("qk", s, i + 1)

            def tables(i, b):
                pool.wait_ge(bias_rows_in[b], 32 * (i + 1))
                mask = col_mask[:, None, :]
                pool.tensor_tensor(bias_full[:, b, 1:REL], bias_full[:, b, 1:REL],
                                   mask.to_broadcast([P, REL - 1, GRID_W]), ALU.add).then_inc(bias_masked, 1)
                pool.wait_ge(bias_masked, 2 * i + b + 1)
                e0 = WIN_ROWS // 2 - 1
                pool.tensor_tensor(bias_inner[:, b], bias_full[:, b, e0:e0 + WIN_ROWS + 1], row_mask[:],
                                   ALU.add).then_inc(bias_done, 1)

            def normalise(i, u, ab):
                n, pb = 16 * i + 2 * u + ab, 2 * (u % 2) + ab
                keys = TC + unit_row(u, ab)[1] * GRID_W
                pool.wait_ge(inv_done, n + 1)
                pool.sem_inc(pool_passed, 1)
                pool.tensor_scalar(probs[:, pb, 0:keys], probs[:, pb, 0:keys], stats[:, pb, 3:4], 1.0,
                                   ALU.mult, ALU.mult).then_inc(probs_done, 1)

            def out_low(i, u, started):
                h0, q0 = DH * (u // 4), 4 * (u % 4) * GRID_W
                if h0:
                    pool.wait_ge(probs_done, started)
                pool.wait_ge(o_hi_done, UNITS * i + u + 1)
                pool.tensor_tensor(o_lo[h0:h0 + DH, i, q0:q0 + 2 * P], o_sum[h0:h0 + DH, :],
                                   o_hi[h0:h0 + DH, i, q0:q0 + 2 * P], ALU.subtract).then_inc(o_lo_done, 1)
                if h0:
                    pool.wait_ge(o_lo_done, UNITS * i + u + 1)

            def attention(i, last):
                first = isinstance(i, int) and i == 0
                for u in range(UNITS):
                    nxt_i, nxt_u = (i, u + 1) if u < UNITS - 1 else (i + 1, 0)
                    if u == 0:
                        tables(i, 1)
                    if u == 4 and not last:
                        tables(i + 1, 0)
                        pool.wait_ge(bias_done, 2 * i + 3)
                    more = not (last and u == UNITS - 1)
                    if more:
                        normalise(nxt_i, nxt_u, 0)
                        normalise(nxt_i, nxt_u, 1)
                    if not (first and u == 0):
                        out_low(*before(i, u), 16 * i + 2 * u + (4 if more else 2))
            tables(0, 0)
            normalise(0, 0, 0)
            normalise(0, 0, 1)
            attention(0, False)
            with pool.Fori(1, PAIRS - 1) as i:
                attention(i, False)
            attention(PAIRS - 1, True)
            out_low(PAIRS - 1, UNITS - 1, 2 * UNITS * PAIRS)

            for s in range(4):
                split_lo("wo", s, 0)
            for p in range(PAIRS - 2):
                split_lo("wo", p % 4, p // 4 + 1)
            norm(3, LAT)
            with pool.Fori(0, HIDDEN - 1) as j:
                ffn_step("ffn1", j)
            ffn_step("ffn1", HIDDEN - 1, last=True)


def kernel(x, c, ctx, c_ctx, mod_w, mod_b, mix_norm_g, ffn_norm_g, conv_w_in, conv_w, conv_w_out, nat_w_qkv,
           nat_rpb, nat_w_o, mla_w_dq, mla_q_norm_g, mla_w_uq, mla_w_dkv, mla_kv_norm_g, mla_w_ukv, mla_w_o,
           fnet_w_o, ffn_w_in, ffn_w_out, final_norm_g):
    import numpy as np
    from concourse import bacc
    from concourse.bass_utils import run_bass_kernel_spmd

    arr = {n: np.asarray(a) for n, a in dict(
        x=x, c=c, ctx=ctx, c_ctx=c_ctx, mod_w=mod_w, mod_b=mod_b, mix_norm_g=mix_norm_g, ffn_norm_g=ffn_norm_g,
        conv_w_in=conv_w_in, conv_w=conv_w, conv_w_out=conv_w_out, nat_w_qkv=nat_w_qkv, nat_rpb=nat_rpb,
        nat_w_o=nat_w_o, ffn_w_in=ffn_w_in, ffn_w_out=ffn_w_out, final_norm_g=final_norm_g).items()}
    D = arr["x"].shape[-1]
    KB = D // P
    TL, TC = arr["x"].shape[1], arr["ctx"].shape[1]
    F = arr["ffn_w_out"].shape[1]

    def columns(w):
        return w.reshape(KB, P, -1, P).transpose(2, 1, 0, 3).reshape(-1, P, D)

    def per_channel(v):
        return np.moveaxis(v.reshape(*v.shape[:-1], KB, P), -1, 0)

    conv_in = columns(arr["conv_w_in"][0]).reshape(3, KB, P, D)
    conv = np.stack([conv_in[1], conv_in[2], conv_in[0], arr["conv_w_out"][0].reshape(KB, P, D)], 1)
    ffn = []
    for layer in range(2):
        up = columns(arr["ffn_w_in"][layer]).reshape(2, F // P, P, D)
        ffn.append(np.stack([up[0], up[1], arr["ffn_w_out"][layer].reshape(F // P, P, D)], 1))
    qkv = columns(arr["nat_w_qkv"][0]).reshape(3, KB, P, D)
    rpb = arr["nat_rpb"][0]
    side = GRID_W - WIN_COLS
    arrays = {
        "x_t": arr["x"][0].T.reshape(KB, P, TL),
        "ctx_t": arr["ctx"][0].T.reshape(KB, P, TC),
        "c_t": per_channel(np.stack([arr["c"][0], arr["c_ctx"]])).transpose(0, 2, 1),
        "mod_panels": columns(arr["mod_w"][0]),
        "mod_rest": arr["mod_w"][1].reshape(KB, P, -1, 3 * P).transpose(2, 0, 1, 3),
        "mod_bias": arr["mod_b"].reshape(-1, P).T,
        "norm_gains": per_channel(np.stack([arr["mix_norm_g"][0], arr["ffn_norm_g"][0], arr["mix_norm_g"][1],
                                            arr["ffn_norm_g"][1], arr["final_norm_g"]])),
        "conv_panels": conv,
        "conv_taps": per_channel(arr["conv_w"][0]),
        "ffn_panels": np.stack(ffn),
        "v_panels": qkv[2],
        "qk_panels": np.stack([qkv[0], qkv[1]], 1),
        "wo_panels": columns(arr["nat_w_o"][0]),
        "rpb_padded": np.pad(rpb, ((0, 0), (0, 0), (side, side))),
    }
    nc = bacc.Bacc("TRN2", target_bir_lowering=False, num_devices=1)
    arrays = {n: np.ascontiguousarray(a) for n, a in arrays.items()}
    args = [nc.dram_tensor(n, a.shape, F32, kind="ExternalInput").ap() for n, a in arrays.items()]
    out = nc.dram_tensor("out_t", (KB, P, TL), F32, kind="ExternalOutput").ap()
    trunk(nc, *args, out)
    r = run_bass_kernel_spmd(nc, [arrays], core_ids=[0])
    return np.ascontiguousarray(r.results[0]["out_t"].reshape(D, TL).T)[None]
```
